# Optimizing a Trainium2 kernel written in Bass

```python
import jax, jax.numpy as jnp
from jax import lax
import numpy as np

D_MODEL = 2048
BATCH = 1
SEQ = 256
DEPTH = 1

D_MIX = 2 * D_MODEL
D_A = D_MIX // 2
CHUNK_A = 128
N_GROUPS_A = 16
D_HEAD_A = D_A // N_GROUPS_A
D_SSM = D_MIX - D_A
SSM_HEAD_DIM = 64
N_SSM_HEADS = D_SSM // SSM_HEAD_DIM
N_SSM_GROUPS = 8
HEADS_PER_GROUP = N_SSM_HEADS // N_SSM_GROUPS
D_STATE = 128
SSM_CONV = 4
SSD_CHUNK = 128
D_XBC = D_SSM + 2 * N_SSM_GROUPS * D_STATE
D_IN = 2 * D_A + D_SSM + D_XBC + N_SSM_HEADS
D_FF = 5632
FFN_CONV = 3
D_PLE = 256
EPS = 1e-6

kernel_name = "hybrid_gmlp_ssd_convffn_ple"

def rms_norm(x, g):
    xf = x.astype(jnp.float32)
    y = xf * lax.rsqrt(jnp.mean(xf * xf, axis=-1, keepdims=True) + EPS)
    return (y * g.astype(jnp.float32)).astype(x.dtype)

def causal_dwconv(x, w, b):
    k_w = w.shape[0]
    s = x.shape[1]
    xp = jnp.pad(x, ((0, 0), (k_w - 1, 0), (0, 0)))
    y = b
    for k in range(k_w):
        y = y + xp[:, k:k + s] * w[k]
    return y

def gmlp_chunk_mixer(uv, ln_g, ln_b, w_s, b_s):
    bn, s, _ = uv.shape
    uv = jax.nn.gelu(uv)
    u, v = jnp.split(uv, 2, axis=-1)
    v = v.reshape(bn, s // CHUNK_A, CHUNK_A, N_GROUPS_A, D_HEAD_A)
    vf = v.astype(jnp.float32)
    mu = jnp.mean(vf, axis=-1, keepdims=True)
    var = jnp.mean(jnp.square(vf - mu), axis=-1, keepdims=True)
    g = ln_g.reshape(N_GROUPS_A, D_HEAD_A).astype(jnp.float32)
    bb = ln_b.reshape(N_GROUPS_A, D_HEAD_A).astype(jnp.float32)
    vn = ((vf - mu) * lax.rsqrt(var + EPS) * g + bb).astype(uv.dtype)
    mask = jnp.tril(jnp.ones((CHUNK_A, CHUNK_A), dtype=bool))
    ws = jnp.where(mask[None], w_s, jnp.zeros_like(w_s))
    sg = jnp.einsum('gts,bcsgd->bctgd', ws, vn) + b_s.T[:, :, None]
    return u * sg.reshape(bn, s, D_A)

def ssd_chunked(xs, dt, a, bm, cm, d_skip):
    bn, s, _ = xs.shape
    nc = s // SSD_CHUNK
    shp = (bn, nc, SSD_CHUNK, N_SSM_GROUPS, HEADS_PER_GROUP)
    x5 = xs.reshape(shp + (SSM_HEAD_DIM,))
    dt5 = dt.reshape(shp)
    b5 = bm.reshape(bn, nc, SSD_CHUNK, N_SSM_GROUPS, D_STATE)
    c5 = cm.reshape(bn, nc, SSD_CHUNK, N_SSM_GROUPS, D_STATE)
    a_dt = dt5 * a.reshape(N_SSM_GROUPS, HEADS_PER_GROUP)
    x_dt = x5 * dt5[..., None]
    a_cs = jnp.cumsum(a_dt, axis=2)
    a_t = jnp.moveaxis(a_cs, 2, -1)
    diff = a_t[..., :, None] - a_t[..., None, :]
    mask = jnp.tril(jnp.ones((SSD_CHUNK, SSD_CHUNK), dtype=bool))
    l_mat = jnp.exp(jnp.where(mask, diff, -jnp.inf))
    scores = jnp.einsum('bclgn,bcsgn->bcgls', c5, b5)
    y_diag = jnp.einsum('bcgrls,bcsgrp->bclgrp', scores[:, :, :, None] * l_mat, x_dt)
    decay_states = jnp.exp(a_cs[:, :, -1:] - a_cs)
    states = jnp.einsum('bclgn,bclgrp->bcgrpn', b5, x_dt * decay_states[..., None])
    chunk_decay = jnp.exp(a_cs[:, :, -1])

    def step(h, inp):
        dec, st = inp
        return dec[..., None, None] * h + st, h

    h0 = jnp.zeros((bn, N_SSM_GROUPS, HEADS_PER_GROUP, SSM_HEAD_DIM, D_STATE), jnp.float32)
    _, h_in = lax.scan(step, h0, (jnp.moveaxis(chunk_decay, 1, 0), jnp.moveaxis(states, 1, 0)))
    h_in = jnp.moveaxis(h_in, 0, 1)
    y_off = jnp.einsum('bclgn,bcgrpn->bclgrp', c5, h_in) * jnp.exp(a_cs)[..., None]
    y = y_diag + y_off + d_skip.reshape(N_SSM_GROUPS, HEADS_PER_GROUP, 1) * x5
    return y.reshape(bn, s, D_SSM)

def mamba2_mixer(z, xbc, dt_raw, conv_w, conv_b, dt_bias, a_log, d_skip, norm_g):
    bn, s, _ = z.shape
    xbc = jax.nn.silu(causal_dwconv(xbc, conv_w, conv_b))
    n_bc = N_SSM_GROUPS * D_STATE
    xs = xbc[..., :D_SSM].astype(jnp.float32)
    bm = xbc[..., D_SSM:D_SSM + n_bc].astype(jnp.float32)
    cm = xbc[..., D_SSM + n_bc:].astype(jnp.float32)
    dt = jax.nn.softplus(dt_raw.astype(jnp.float32) + dt_bias.astype(jnp.float32))
    a = -jnp.exp(a_log.astype(jnp.float32))
    y = ssd_chunked(xs, dt, a, bm, cm, d_skip.astype(jnp.float32))
    y = y * jax.nn.silu(z.astype(jnp.float32))
    yg = y.reshape(bn, s, N_SSM_GROUPS, D_SSM // N_SSM_GROUPS)
    yg = yg * lax.rsqrt(jnp.mean(yg * yg, axis=-1, keepdims=True) + EPS)
    y = yg.reshape(bn, s, D_SSM) * norm_g.astype(jnp.float32)
    return y.astype(z.dtype)

def setup_inputs(seed: int = 0) -> dict:
    key = jax.random.key(seed)
    ks = jax.random.split(key, 32)
    f32 = jnp.float32
    nrm = lambda k, shape, scale: jax.random.normal(k, shape, f32) * scale
    gain = lambda k, n: 1.0 + 0.05 * jax.random.normal(k, (DEPTH, n), f32)
    dt0 = jnp.exp(jax.random.uniform(ks[5], (DEPTH, N_SSM_HEADS), f32,
                                     np.log(1e-3).astype(np.float32), np.log(1e-1).astype(np.float32)))
    dt_bias = dt0 + jnp.log(-jnp.expm1(-dt0))
    return {
        "x": jax.random.normal(ks[0], (BATCH, SEQ, D_MODEL), f32),
        "p": jax.random.normal(ks[1], (DEPTH, BATCH, SEQ, D_PLE), f32),
        "norm_mix_g": gain(ks[2], D_MODEL),
        "w_in": nrm(ks[3], (DEPTH, D_MODEL, D_IN), D_MODEL ** -0.5),
        "ln_a_g": gain(ks[4], D_A),
        "ln_a_b": nrm(ks[6], (DEPTH, D_A), 0.02),
        "w_s": nrm(ks[7], (DEPTH, N_GROUPS_A, CHUNK_A, CHUNK_A), CHUNK_A ** -0.5),
        "b_s": 1.0 + nrm(ks[8], (DEPTH, N_GROUPS_A, CHUNK_A), 0.1),
        "norm_a_g": gain(ks[9], D_A),
        "conv_ssm_w": nrm(ks[10], (DEPTH, SSM_CONV, D_XBC), SSM_CONV ** -0.5),
        "conv_ssm_b": nrm(ks[11], (DEPTH, D_XBC), 0.02),
        "dt_bias": dt_bias,
        "a_log": jnp.log(jax.random.uniform(ks[12], (DEPTH, N_SSM_HEADS), f32, 1.0, 16.0)),
        "d_skip": 1.0 + nrm(ks[13], (DEPTH, N_SSM_HEADS), 0.1),
        "ssm_norm_g": gain(ks[14], D_SSM),
        "w_out": nrm(ks[15], (DEPTH, D_MIX, D_MODEL), D_MIX ** -0.5),
        "norm_ffn_g": gain(ks[16], D_MODEL),
        "w_up": nrm(ks[17], (DEPTH, D_MODEL, 2 * D_FF), D_MODEL ** -0.5),
        "conv_ffn_w": nrm(ks[18], (DEPTH, FFN_CONV, 2 * D_FF), FFN_CONV ** -0.5),
        "conv_ffn_b": nrm(ks[19], (DEPTH, 2 * D_FF), 0.02),
        "w_down": nrm(ks[20], (DEPTH, D_FF, D_MODEL), D_FF ** -0.5),
        "norm_ple_g": gain(ks[21], D_MODEL),
        "w_ple_gate": nrm(ks[22], (DEPTH, D_MODEL, D_MODEL), D_MODEL ** -0.5),
        "w_ple": nrm(ks[23], (DEPTH, D_PLE, D_MODEL), D_PLE ** -0.5),
        "norm_final_g": 1.0 + 0.05 * jax.random.normal(ks[24], (D_MODEL,), f32),
    }

def reference(x, p, norm_mix_g, w_in, ln_a_g, ln_a_b, w_s, b_s, norm_a_g,
              conv_ssm_w, conv_ssm_b, dt_bias, a_log, d_skip, ssm_norm_g, w_out,
              norm_ffn_g, w_up, conv_ffn_w, conv_ffn_b, w_down,
              norm_ple_g, w_ple_gate, w_ple, norm_final_g):
    h = x
    o_z = 2 * D_A
    o_xbc = o_z + D_SSM
    o_dt = o_xbc + D_XBC
    for i in range(DEPTH):
        a = rms_norm(h, norm_mix_g[i])
        proj = a @ w_in[i]
        y_a = gmlp_chunk_mixer(proj[..., :o_z], ln_a_g[i], ln_a_b[i], w_s[i], b_s[i])
        y_a = rms_norm(y_a, norm_a_g[i])
        y_b = mamba2_mixer(proj[..., o_z:o_xbc], proj[..., o_xbc:o_dt], proj[..., o_dt:],
                           conv_ssm_w[i], conv_ssm_b[i], dt_bias[i], a_log[i], d_skip[i],
                           ssm_norm_g[i])
        h = h + jnp.concatenate([y_a, y_b], axis=-1) @ w_out[i]
        f = rms_norm(h, norm_ffn_g[i])
        hid = causal_dwconv(f @ w_up[i], conv_ffn_w[i], conv_ffn_b[i])
        gate, up = jnp.split(hid, 2, axis=-1)
        h = h + (jax.nn.silu(gate) * up) @ w_down[i]
        g_ple = jax.nn.sigmoid(rms_norm(h, norm_ple_g[i]) @ w_ple_gate[i])
        h = h + g_ple * (p[i] @ w_ple[i])
    return rms_norm(h, norm_final_g)


_drawn_inputs = setup_inputs


def setup_inputs(seed=0):
    import zlib

    import numpy as np

    out = dict(_drawn_inputs(seed))
    spreads = {}
    factors = {'ln_a_g': 4.049,
     'ln_a_b': 22.097,
     'conv_ssm_b': 4.062,
     'conv_ffn_b': 5.389,
     'norm_ple_g': 8.0}
    for name, (base, spread) in spreads.items():
        noise = np.random.default_rng([zlib.crc32(name.encode()), seed]).standard_normal(out[name].shape)
        drawn = base * np.exp(spread * noise) if base else spread * noise
        out[name] = __import__('jax').numpy.asarray(drawn.astype(out[name].dtype))
    for name, factor in factors.items():
        out[name] = (out[name] * factor).astype(out[name].dtype)
    return out
```

```python
from contextlib import ExitStack

import concourse.bass as bass
from concourse import mybir

F32 = mybir.dt.float32
F32R = mybir.dt.float32r
ALU = mybir.AluOpType
ACT = mybir.ActivationFunctionType
AX = mybir.AxisListType

P = 128
SEQ = 256
NT = SEQ // P
D = 2048
KD = D // P
NB = 512
NBLK = D // NB
BT = NB // P
GROUPS = 8
HPG = 4
HD = 64
GC = HPG * HD
HEADS = GROUPS * HPG
D_FF = 5632
KF = D_FF // P
FB = D_FF // NB
D_PLE = 256
EPS = 1e-6

KC = 2
SLOTS = 4
CB = KD // KC
CF = KF // KC

Z0 = 0
G0 = Z0 + NBLK
V0 = G0 + GROUPS
O0 = V0 + 2 * NBLK
F0 = O0 + 2 * NBLK
CHUNK_D = (F0 + 2 * FB) * CB
CHUNK_P = CHUNK_D + NBLK * CF
CHUNK_E = CHUNK_P + NBLK
CHUNKS = CHUNK_E + NBLK * CB
AHEAD = 12

A_Z, A_VU, A_P, A_E = 0, 4, 12, 16
V_G, V_O, V_F, V_D = 0, 8, 16, 38

C_MIX, C_FFN, C_PLE, C_A, C_SSM, C_BS = 0, 16, 32, 48, 64, 80
C_CONV = 96
C_CONVF = C_CONV + GROUPS * BT * 5
N_PRM = C_CONVF + 2 * KF * 4


class Order:

    def __init__(self, sem):
        self.sem, self.n, self.i, self.per = sem, 0, 0, 0

    def mark(self, instruction):
        instruction.then_inc(self.sem, 1)
        self.n += 1

    def wait(self, engine):
        engine.wait_ge(self.sem, self.n + self.per * self.i)

    def enter(self, i, per):
        self.i, self.per, self.start = i, per, self.n

    def leave(self, times):
        assert self.n - self.start == self.per, (self.n - self.start, self.per)
        self.n, self.i, self.per = self.start + self.per * times, 0, 0


def build(nc, x, xT, wstream, wdt, prm_d, rows_d, wsT_d, ln_d, pT_d, gf_d, out):
    ctx = ExitStack()
    with ctx:
        def sb(stack, name, shape, dt=F32):
            return stack.enter_context(nc.sbuf_tensor(name, shape, dt))

        def sem(name):
            return ctx.enter_context(nc.semaphore(name))

        h = sb(ctx, "h", [P, NT * D])
        h3 = h[:, :].rearrange("p (t d) -> p t d", t=NT)
        aH = sb(ctx, "aH", [P, KD, SEQ], F32R)
        aL = sb(ctx, "aL", [P, KD, SEQ], F32R)
        raw = sb(ctx, "raw", [P, SLOTS, KC, NB])
        wH = sb(ctx, "wH", [P, SLOTS, KC, NB], F32R)
        wL = sb(ctx, "wL", [P, SLOTS, KC, NB], F32R)
        prm = sb(ctx, "prm", [P, N_PRM])
        ident = sb(ctx, "ident", [P, P])
        ones = sb(ctx, "ones", [P, P])
        rb = sb(ctx, "rb", [P, SEQ])
        dg = sb(ctx, "dg", [P, NT, P])
        small = sb(ctx, "small", [P, 512])
        at = [0]

        def cols(n, *shape):
            v = small[:, at[0]:at[0] + n]
            at[0] += n
            assert at[0] <= 512
            if len(shape) == 2:
                v = v.rearrange("p (a b) -> p a b", b=shape[1])
            return v

        half, eps, inv_d, inv_g = (cols(8) for _ in range(4))
        ss0, r0 = cols(2), cols(2)
        ssA, sA, rA = cols(8, NT, NBLK), cols(2), cols(2)
        ssH, sH, rH = cols(8, NT, NBLK), cols(2), cols(2)
        ssP, sP, rP = cols(8, NT, NBLK), cols(2), cols(2)
        ssF, sF, rF = cols(8, NT, NBLK), cols(2), cols(2)
        ssG, rG = cols(2), cols(2)
        mv, rs, nm = cols(16, 8, 2), cols(8), cols(8)
        bst = cols(48, 8, 6)

        z4 = h[:, :].rearrange("p (g t c) -> p g t c", g=GROUPS, t=NT)
        v = h[:, 0:1024].rearrange("p (t c) -> p t c", t=NT)
        u = h[:, 1024:2048].rearrange("p (t c) -> p t c", t=NT)
        wsT = h[:, 2048:2560].rearrange("p (g t) -> p g t", g=BT)
        lnr = h[:, 2560:3584].rearrange("p (a c) -> p a c", a=2)

        mix = ExitStack()
        yBH = sb(mix, "yBH", [P, KD, SEQ], F32R)
        yBL = sb(mix, "yBL", [P, KD, SEQ], F32R)
        yAH = sb(mix, "yAH", [P, KD, SEQ], F32R)
        yAL = sb(mix, "yAL", [P, KD, SEQ], F32R)
        upper = sb(mix, "upper", [P, P])
        lower = sb(mix, "lower", [P, P])
        rows = sb(mix, "rows", [P, 3, HEADS])
        dts = sb(mix, "dts", [P, 8, NT * HEADS])
        dt, adt, ea, acc, sq_, dtu, dte, dtq = (dts[:, n, :] for n in range(8))
        ed = sb(mix, "ed", [P, HEADS])
        start = ExitStack()
        xTs = sb(start, "xTs", [P, KD, SEQ])
        wdtr = sb(start, "wdtr", [P, KD, HEADS])
        wdtH = sb(start, "wdtH", [P, KD, HEADS], F32R)
        wdtL = sb(start, "wdtL", [P, KD, HEADS], F32R)
        start.close()
        xs = sb(mix, "xs", [P, BT, 3 + SEQ])
        cv = sb(mix, "cv", [P, BT, SEQ])
        xtok = sb(mix, "xtok", [P, NT, GC])
        btok = sb(mix, "btok", [P, P])
        xdt = sb(mix, "xdt", [P, NT, GC])
        xdd = sb(mix, "xdd", [P, GC])
        ld = sb(mix, "ld", [P, NT, HPG, P])
        sc = sb(mix, "sc", [P, NT, P])
        E = sb(mix, "E", [P, NT, HPG, P])
        stT = sb(mix, "stT", [P, GC])
        yx = sb(mix, "yx", [P, NT, GC])
        y = sb(mix, "y", [P, NT, GC])
        yo = sb(mix, "yo", [P, GC])
        mix.close()

        ffn = ExitStack()
        guH = sb(ffn, "guH", [P, KF, SEQ], F32R)
        guL = sb(ffn, "guL", [P, KF, SEQ], F32R)
        xf = sb(ffn, "xf", [P, BT, 2 + SEQ])
        cfG = sb(ffn, "cfG", [P, BT, SEQ])
        cfU = sb(ffn, "cfU", [P, BT, SEQ])
        pH = sb(ffn, "pH", [P, KC, SEQ], F32R)
        pL = sb(ffn, "pL", [P, KC, SEQ], F32R)
        hb = cfU[:, :, :].rearrange("p (t a) c -> p t (a c)", t=NT)
        junk = cfG[:, :, :].rearrange("p (t a) c -> p t (a c)", t=NT)
        praw = xf[:, 0:KC, 2:2 + SEQ]
        ffn.close()
        last = ExitStack()
        pw = sb(last, "pw", [P, NT, D])
        gate = sb(last, "gate", [P, NT, NB])
        gf = sb(last, "gf", [P, D])
        last.close()

        ps = [ctx.enter_context(nc.psum_tensor(f"ps{n}", [P, NB], F32)) for n in range(8)]

        def tok_bank(block, t):
            return ps[2 * (block % 2) + t]

        raw_in = [sem(f"raw_in{j}") for j in range(SLOTS)]
        wh_ready, wl_ready, chunk_used = sem("wh_ready"), sem("wl_ready"), sem("chunk_used")
        act_evac, dve_evac = sem("act_evac"), sem("dve_evac")
        xT_in = [sem(f"xT_in{j}") for j in range(4)]
        prm_in, rows_in, x_in, wdt_in, x2_in = (sem(n) for n in ("prm_in", "rows_in", "x_in", "wdt_in", "x2_in"))
        const_ready, masks_ready = sem("const_ready"), sem("masks_ready")
        ah_ready, al_ready = sem("ah_ready"), sem("al_ready")
        ss0_ready, r0_ready, dg_ready, rbmm_done, rb_ready = (
            sem(n) for n in ("ss0_ready", "r0_ready", "dg_ready", "rbmm_done", "rb_ready"))
        wdth_ready, wdtl_ready, dtmm_done, csmm_done = (
            sem(n) for n in ("wdth_ready", "wdtl_ready", "dtmm_done", "csmm_done"))
        dtu_ready, dte_ready, adt_ready, ea_ready = (
            sem(n) for n in ("dtu_ready", "dte_ready", "adt_ready", "ea_ready"))
        cv0_ready, conv_ready, silu_ready = sem("cv0_ready"), sem("conv_ready"), sem("silu_ready")
        ld_ready, diff_done, exp_ready = sem("ld_ready"), sem("diff_done"), sem("exp_ready")
        xtr_done, scores_done, tok_ready = sem("xtr_done"), sem("scores_done"), sem("tok_ready")
        btok_ready = sem("btok_ready")
        xd_ready, yx_ready, st_done, st_ready = sem("xd_ready"), sem("yx_ready"), sem("st_done"), sem("st_ready")
        m_ready, y_done, y_ready = sem("m_ready"), sem("y_done"), sem("y_ready")
        ssg_ready, rg_ready, yn_ready = sem("ssg_ready"), sem("rg_ready"), sem("yn_ready")
        ytr_done, yh_ready, yl_ready = sem("ytr_done"), sem("yh_ready"), sem("yl_ready")
        ws_in, ws_ready, mv_ready, rs_ready, vn_ready = (
            sem(n) for n in ("ws_in", "ws_ready", "mv_ready", "rs_ready", "vn_ready"))
        sg_done, ya_ready, ssa_ready, yatr_done, yah_ready, yal_ready = (
            sem(n) for n in ("sg_done", "ya_ready", "ssa_ready", "yatr_done", "yah_ready", "yal_ready"))
        sa_ready, ra_ready = sem("sa_ready"), sem("ra_ready")
        hcopy_done, ssh_ready, htr_done, fh_ready, fl_ready = (
            sem(n) for n in ("hcopy_done", "ssh_ready", "htr_done", "fh_ready", "fl_ready"))
        sh_ready, rh_ready = sem("sh_ready"), sem("rh_ready")
        pads_ready, fpads_ready = sem("pads_ready"), sem("fpads_ready")
        fc0_ready, fconv_ready, fsilu_ready, gu_ready, guh_ready, gul_ready = (
            sem(n) for n in ("fc0_ready", "fconv_ready", "fsilu_ready", "gu_ready", "guh_ready", "gul_ready"))
        p_in, ph_ready, pl_ready, gf_in = sem("p_in"), sem("ph_ready"), sem("pl_ready"), sem("gf_in")
        ssp_ready, sp_ready, rp_ready = sem("ssp_ready"), sem("sp_ready"), sem("rp_ready")
        hf_ready, ssf_ready, sf_ready, rf_ready, out_ready, stored = (
            sem(n) for n in ("hf_ready", "ssf_ready", "sf_ready", "rf_ready", "out_ready", "stored"))
        by_tensor = (y_done, sg_done, diff_done)
        by_vector = (y_ready, yl_ready, gul_ready, yal_ready, fl_ready, dve_evac)
        by_scalar = (st_ready, ssh_ready)
        by_gpsimd = (yx_ready, hcopy_done)
        act_order, dve_order, pool_order = Order(sem("act_order")), Order(sem("dve_order")), Order(sem("pool_order"))

        block = ctx.enter_context(nc.Block())

        @block.sync
        def _(sp):
            for j in range(SLOTS):
                sp.dma_start(raw[:, j, :, :], wstream[j]).then_inc(raw_in[j], 16)
            sp.dma_start(wdtr[:, :, :], wdt).then_inc(wdt_in, 16)
            with sp.Fori(1, CHUNKS // SLOTS) as r:
                for j in range(SLOTS):
                    sp.wait_ge(wl_ready, r * SLOTS + (j + 1 - SLOTS))
                    sp.dma_start(raw[:, j, :, :], wstream[r * SLOTS + j]).then_inc(raw_in[j], 16)
            for t in range(NT):
                sp.wait_ge(out_ready, t + 1)
                sp.dma_start(out[t * P:(t + 1) * P, :], h3[:, t, :]).then_inc(stored, 16)
            sp.wait_ge(stored, 16 * NT)

        @block.gpsimd
        def _(pool):
            for first in by_gpsimd:
                pool.sem_inc(first, 1)
            tt = pool.tensor_tensor
            order = pool_order

            def rsqrt(dst, src, inverse, done):
                order.mark(tt(dst, src, inverse[:, 0:NT], ALU.mult))
                order.wait(pool)
                order.mark(tt(dst, dst, eps[:, 0:NT], ALU.add))
                order.wait(pool)
                tt(dst, dst, half[:, 0:NT], ALU.pow).then_inc(done, 1)

            pool.memset(eps, EPS).then_inc(const_ready, 1)
            pool.memset(inv_d, 1.0 / D).then_inc(const_ready, 1)
            pool.memset(inv_g, 1.0 / GC).then_inc(const_ready, 1)
            pool.memset(half, -0.5).then_inc(const_ready, 1)
            pool.memset(ones[:, :], 1.0).then_inc(const_ready, 1)
            pool.memset(ident[:, :], 0.0).then_inc(const_ready, 1)
            pool.wait_ge(const_ready, 6)
            pool.affine_select(out=ident[:, :], in_=ident[:, :], compare_op=ALU.not_equal, fill=1.0, base=0,
                               pattern=[[-1, P]], channel_multiplier=1).then_inc(const_ready, 1)
            pool.affine_select(out=upper[:, :], in_=ones[:, :], compare_op=ALU.is_ge, fill=0.0, base=0,
                               pattern=[[1, P]], channel_multiplier=-1).then_inc(masks_ready, 1)
            pool.affine_select(out=lower[:, :], in_=ones[:, :], compare_op=ALU.is_ge, fill=0.0, base=-1,
                               pattern=[[-1, P]], channel_multiplier=1).then_inc(masks_ready, 1)
            pool.wait_ge(ss0_ready, 1)
            rsqrt(r0, ss0, inv_d, r0_ready)
            pool.wait_ge(r0_ready, 1)
            pool.wait_ge(const_ready, 7)
            for t in range(NT):
                pool.tensor_scalar(dg[:, t, :], ident[:, :], r0[:, t:t + 1], None, ALU.mult).then_inc(dg_ready, 1)
            pool.wait_ge(dtmm_done, 1)
            pool.memset(xs[:, :, 0:3], 0.0).then_inc(pads_ready, 1)
            pool.wait_ge(adt_ready, 1)
            pool.wait_ge(ea_ready, 1)
            with pool.Fori(0, GROUPS) as g:
                order.enter(g, 3)
                pool.wait_ge(diff_done, g * 2 + 1)
                for c in range(NT):
                    a_c = adt[:, bass.ds(g * HPG + c * HEADS, HPG)].unsqueeze(2).broadcast_to([P, HPG, P])
                    tt(ld[:, c, :, :], lower[:, :].unsqueeze(1).broadcast_to([P, HPG, P]), a_c,
                       ALU.mult).then_inc(ld_ready, 1)
                pool.wait_ge(tok_ready, g + 1)
                pool.wait_ge(y_done, g + 1)
                for c in range(NT):
                    d_c = dt[:, bass.ds(g * HPG + c * HEADS, HPG)].unsqueeze(2).broadcast_to([P, HPG, HD])
                    ins = tt(xdt[:, c, :].rearrange("p (h e) -> p h e", h=HPG),
                             xtok[:, c, :].rearrange("p (h e) -> p h e", h=HPG), d_c, ALU.mult)
                    if c == 0:
                        order.mark(ins)
                order.wait(pool)
                tt(xdd[:, :].rearrange("p (h e) -> p h e", h=HPG),
                   xdt[:, 0, :].rearrange("p (h e) -> p h e", h=HPG),
                   ed[:, bass.ds(g * HPG, HPG)].unsqueeze(2).broadcast_to([P, HPG, HD]),
                   ALU.mult).then_inc(xd_ready, 1)
                pool.wait_ge(y_ready, g + 1)
                skip = rows[:, 2, bass.ds(g * HPG, HPG)].unsqueeze(2).broadcast_to([P, HPG, HD])
                for c in range(NT):
                    ins = tt(yx[:, c, :].rearrange("p (h e) -> p h e", h=HPG),
                             xtok[:, c, :].rearrange("p (h e) -> p h e", h=HPG), skip, ALU.mult)
                ins.then_inc(yx_ready, 1)
                pool.wait_ge(ssg_ready, g + 1)
                rsqrt(rG, ssG, inv_g, rg_ready)
            order.leave(GROUPS)
            with pool.Fori(0, NBLK) as i:
                order.enter(i, 1)
                pool.wait_ge(ws_in, i * 32 + 32)
                pool.wait_ge(mv_ready, i + 1)
                order.mark(tt(rs, mv[:, :, 1], eps, ALU.add))
                order.wait(pool)
                tt(rs, rs, half, ALU.pow).then_inc(rs_ready, 1)
                pool.wait_ge(rs_ready, i * 2 + 1)
                tt(nm, mv[:, :, 0], rs, ALU.mult).then_inc(rs_ready, 1)
                pool.affine_select(out=wsT, in_=wsT, compare_op=ALU.is_ge, fill=0.0, base=0,
                                   pattern=[[0, BT], [1, P]], channel_multiplier=-1).then_inc(ws_ready, 1)
            order.leave(NBLK)
            pool.wait_ge(sa_ready, 1)
            rsqrt(rA, sA, inv_d, ra_ready)
            with pool.Fori(0, NBLK) as n:
                pool.wait_ge(dve_evac, n * 2 + (V_O + 2) + 1)
                pool.tensor_copy(h3[:, :, bass.ds(n * NB, NB)], hb).then_inc(hcopy_done, 1)
            pool.memset(xf[:, :, 0:2], 0.0).then_inc(fpads_ready, 1)
            pool.wait_ge(sh_ready, 1)
            rsqrt(rH, sH, inv_d, rh_ready)
            pool.wait_ge(rh_ready, 1)
            for t in range(NT):
                pool.tensor_scalar(dg[:, t, :], ident[:, :], rH[:, t:t + 1], None, ALU.mult).then_inc(dg_ready, 1)
            with pool.Fori(0, NBLK // 2) as i:
                pool.wait_ge(dve_evac, i * 2 + (V_D + 1) + 1)
                pool.tensor_copy(h3[:, :, bass.ds(i * 2 * NB, NB)], hb).then_inc(hcopy_done, 1)
            pool.wait_ge(sp_ready, 1)
            rsqrt(rP, sP, inv_d, rp_ready)
            pool.wait_ge(sf_ready, 1)
            rsqrt(rF, sF, inv_d, rf_ready)

        @block.scalar
        def _(act):
            for first in by_scalar:
                act.sem_inc(first, 1)
            fn = act.activation
            order = act_order

            def split(r, j):
                act.wait_ge(raw_in[j], r * 16 + 16)
                act.wait_ge(chunk_used, r * SLOTS + (j + 1 - SLOTS))
                fn(wH[:, j, :, :], raw[:, j, :, :], ACT.Copy).then_inc(wh_ready, 1)

            def splits(lo, hi):
                while lo < hi:
                    if lo % SLOTS == 0 and hi - lo >= 2 * SLOTS:
                        with act.Fori(lo // SLOTS, hi // SLOTS) as r:
                            for j in range(SLOTS):
                                split(r, j)
                        lo = hi // SLOTS * SLOTS
                    else:
                        split(lo // SLOTS, lo % SLOTS)
                        lo += 1

            def evac_high(dst, banks, k0, col):
                for m in range(BT):
                    ins = fn(dst[:, bass.ds(k0 + m, 1), :].rearrange("p a c -> p (a c)"),
                             ps[banks + m // 2][:, (m % 2) * SEQ:(m % 2 + 1) * SEQ], ACT.Copy,
                             scale=prm[:, bass.ds(k0 + (col + m), 1)])
                return ins

            for j in range(4):
                act.dma_start(xTs[:, 4 * j:4 * j + 4, :], xT[:, 4 * j:4 * j + 4, :]).then_inc(xT_in[j], 16)
                if j == 0:
                    act.dma_start(prm[:, :], prm_d).then_inc(prm_in, 16)
            act.dma_start(h3, x.rearrange("(t p) d -> p t d", p=P)).then_inc(x_in, 16)
            act.dma_start(rows[:, :, :], rows_d.partition_broadcast(P)).then_inc(rows_in, 16)
            act.wait_ge(prm_in, 16)
            for k in range(KD):
                if k % 4 == 0:
                    act.wait_ge(xT_in[k // 4], 16)
                fn(aH[:, k, :], xTs[:, k, :], ACT.Copy, scale=prm[:, C_MIX + k:C_MIX + k + 1]).then_inc(ah_ready, 1)
                if k % 2 == 1:
                    j = k // 2 % SLOTS
                    if k < 2 * SLOTS:
                        act.wait_ge(raw_in[j], 16)
                        fn(wH[:, j, :, :], raw[:, j, :, :], ACT.Copy).then_inc(wh_ready, 1)
                    else:
                        split(1, j)
            act.wait_ge(x_in, 16)
            act.wait_ge(al_ready, KD)
            for t in range(NT):
                ins = fn(xTs[:, t * 8:t * 8 + 8, :].rearrange("p a b -> p (a b)"), h3[:, t, :], ACT.Square,
                         accum_out=ss0[:, t:t + 1])
            ins.then_inc(ss0_ready, 1)
            act.wait_ge(wdt_in, 16)
            fn(wdtH[:, :, :], wdtr[:, :, :], ACT.Copy).then_inc(wdth_ready, 1)
            for j in range(SLOTS):
                split(2, j)

            act.wait_ge(r0_ready, 1)
            for b in range(NBLK):
                q0 = AHEAD + b * CB
                act.wait_ge(chunk_used, (b + 1) * CB)
                for t in range(NT):
                    ins = fn(z4[:, 2 * b:2 * b + 2, t, :], tok_bank(b, t)[:, :].rearrange("p (g c) -> p g c", g=2),
                             ACT.Silu, scale=r0[:, t:t + 1])
                ins.then_inc(act_evac, 1)
                if b < NBLK - 1:
                    splits(q0, q0 + CB)
                    continue
                act.wait_ge(rbmm_done, 1)
                fn(rb[:, :], ps[6][:, 0:SEQ], ACT.Copy).then_inc(rb_ready, 1)
                act.wait_ge(dtu_ready, 1)
                order.mark(fn(dte, dtu, ACT.Abs))
                act.wait_ge(rows_in, 16)
                order.wait(act)
                fn(dte, dte, ACT.Exp, scale=-1.0).then_inc(dte_ready, 1)
                fn(rows[:, 1, :], rows[:, 1, :], ACT.Exp).then_inc(dte_ready, 1)
                splits(q0, q0 + CB - 2)
                act.wait_ge(csmm_done, 1)
                fn(ea, ps[7][:, 0:NT * HEADS], ACT.Exp)
                fn(ed[:, :], ps[7][:, P:P + HEADS], ACT.Exp).then_inc(ea_ready, 1)
                splits(q0 + CB - 2, q0 + CB)

            with act.Fori(0, GROUPS // 2) as i:
                for b in range(2):
                    g = i * 2 + b

                    def s(c):
                        split(i * 4 + (3 + 2 * G0 + 2 * b + c // 4), c % 4)

                    act.wait_ge(dve_evac, g + (V_G + 1) + 1)
                    act.wait_ge(y_done, g + 1)
                    for m in range(BT):
                        w = C_CONV + 5 * m
                        ins = fn(cv[:, m, :], xs[:, m, 3:3 + SEQ], ACT.Identity,
                                 scale=prm[:, bass.ds(g * (5 * BT) + (w + 3), 1)],
                                 bias=prm[:, bass.ds(g * (5 * BT) + (w + 4), 1)])
                    ins.then_inc(cv0_ready, 1)
                    s(0)
                    for c in range(NT):
                        act.wait_ge(diff_done, g * 2 + (c + 1) + 1)
                        fn(E[:, c, :, :].rearrange("p h l -> p (h l)"), ps[6 + c][:, :], ACT.Exp).then_inc(exp_ready, 1)
                    s(1)
                    s(2)
                    act.wait_ge(conv_ready, g + 1)
                    fn(cv[:, :, :], cv[:, :, :], ACT.Silu).then_inc(silu_ready, 1)
                    s(3)
                    act.wait_ge(xtr_done, g + 1)
                    act.wait_ge(yx_ready, g + 1)
                    fn(xtok[:, :, :].rearrange("p t c -> p (t c)"), ps[4][:, :], ACT.Copy).then_inc(tok_ready, 1)
                    s(4)
                    act.wait_ge(st_done, g + 1)
                    fn(stT[:, :], ps[4][:, 0:GC], ACT.Copy).then_inc(st_ready, 1)
                    s(5)
                    s(6)
                    act.wait_ge(y_ready, g + 1 + 1)
                    for t in range(NT):
                        ins = fn(xs[:, t, 3:3 + GC], y[:, t, :], ACT.Square, accum_out=ssG[:, t:t + 1])
                    ins.then_inc(ssg_ready, 1)
                    act.wait_ge(rg_ready, g + 1)
                    for t in range(NT):
                        ins = fn(y[:, t, :], y[:, t, :], ACT.Copy, scale=rG[:, t:t + 1])
                    ins.then_inc(yn_ready, 1)
                    s(7)
                    act.wait_ge(ytr_done, g + 1)
                    for m in range(2):
                        ins = fn(yBH[:, bass.ds(g * 2 + m, 1), :].rearrange("p a c -> p (a c)"),
                                 ps[5][:, m * SEQ:(m + 1) * SEQ], ACT.Copy,
                                 scale=prm[:, bass.ds(g * 2 + (C_SSM + m), 1)])
                    ins.then_inc(yh_ready, 1)

            with act.Fori(0, NBLK) as i:
                def s(lo, hi):
                    for c in range(lo, hi):
                        split(i * 4 + (3 + 2 * V0 + c // 4), c % 4)

                act.wait_ge(chunk_used, i * (2 * CB) + (V0 + 1) * CB)
                act.wait_ge(sg_done, i + 1)
                act.dma_start(wsT, wsT_d[i]).then_inc(ws_in, 16)
                act.dma_start(lnr, ln_d[i].partition_broadcast(P)).then_inc(ws_in, 16)
                for t in range(NT):
                    ins = fn(v[:, t, :], tok_bank(0, t)[:, :], ACT.Gelu_apprx_tanh, scale=r0[:, t:t + 1])
                ins.then_inc(act_evac, 1)
                s(0, CB)
                act.wait_ge(chunk_used, i * (2 * CB) + (V0 + 2) * CB)
                for t in range(NT):
                    ins = fn(u[:, t, :], tok_bank(1, t)[:, :], ACT.Gelu_apprx_tanh, scale=r0[:, t:t + 1])
                ins.then_inc(act_evac, 1)
                s(CB, CB + 3)
                act.wait_ge(ya_ready, i + 1)
                for t in range(NT):
                    ins = fn(v[:, t, :], u[:, t, :], ACT.Square, accum_out=ssA[:, t, bass.ds(i, 1)])
                ins.then_inc(ssa_ready, 1)
                s(CB + 3, CB + 5)
                act.wait_ge(yatr_done, i + 1)
                evac_high(yAH, 6, i * BT, C_A).then_inc(yah_ready, 1)
                s(CB + 5, 2 * CB)

            act.wait_ge(ssa_ready, NBLK)
            act.dma_start(h3, x.rearrange("(t p) d -> p t d", p=P)).then_inc(x2_in, 16)

            with act.Fori(0, NBLK) as n:
                def s(lo, hi):
                    for c in range(lo, hi):
                        split(n * 4 + (3 + 2 * O0 + c // 4), c % 4)

                s(0, CB + 1)
                act.wait_ge(dve_evac, n * 2 + (V_O + 2) + 1)
                for t in range(NT):
                    ins = fn(junk[:, t, :], hb[:, t, :], ACT.Square, accum_out=ssH[:, t, bass.ds(n, 1)])
                ins.then_inc(ssh_ready, 1)
                s(CB + 1, CB + 3)
                act.wait_ge(htr_done, n + 1)
                evac_high(aH, 4, n * BT, C_FFN).then_inc(fh_ready, 1)
                s(CB + 3, 2 * CB)
            act.wait_ge(rbmm_done, 2)
            fn(rb[:, :], ps[6][:, 0:SEQ], ACT.Copy).then_inc(rb_ready, 1)

            act.wait_ge(hcopy_done, NBLK + 1)
            with act.Fori(0, FB) as i:
                for b, cf in enumerate((cfG, cfU)):
                    def s(lo, hi):
                        for c in range(lo, hi):
                            split(i * 4 + (3 + 2 * F0 + 2 * b + c // 4), c % 4)

                    s(0, 1)
                    act.wait_ge(dve_evac, i * 2 + (V_F + 1 + b) + 1)
                    act.wait_ge(gul_ready, i + 1)
                    for m in range(BT):
                        w = C_CONVF + 4 * (m + b * KF)
                        ins = fn(cf[:, m, :], xf[:, m, 2:2 + SEQ], ACT.Identity,
                                 scale=prm[:, bass.ds(i * (4 * BT) + (w + 2), 1)],
                                 bias=prm[:, bass.ds(i * (4 * BT) + (w + 3), 1)])
                    ins.then_inc(fc0_ready, 1)
                    s(1, 4)
                    if b == 0:
                        act.wait_ge(fconv_ready, i * 2 + 1)
                        fn(cfG[:, :, :], cfG[:, :, :], ACT.Silu).then_inc(fsilu_ready, 1)
                        s(4, 8)
                    else:
                        s(4, 5)
                        act.wait_ge(gu_ready, i + 1)
                        fn(guH[:, bass.ds(i * BT, BT), :], cfU[:, :, :], ACT.Copy).then_inc(guh_ready, 1)
                        s(5, 8)

            act.wait_ge(fconv_ready, 2 * FB)
            act.dma_start(praw, pT_d).then_inc(p_in, 16)
            q = CHUNK_D + AHEAD
            splits(q, q + 4)
            act.wait_ge(p_in, 16)
            fn(pH[:, :, :], praw, ACT.Copy).then_inc(ph_ready, 1)
            splits(q + 4, CHUNK_D + CF + SLOTS)

            for n in range(NBLK):
                q = CHUNK_D + (n + 1) * CF + SLOTS
                splits(q, q + 1)
                act.wait_ge(dve_evac, V_D + 1 + n + 1)
                for t in range(NT):
                    src = h3[:, t, n * NB:(n + 1) * NB] if n % 2 else hb[:, t, :]
                    ins = fn(junk[:, t, :], src, ACT.Square, accum_out=ssP[:, t, n:n + 1])
                ins.then_inc(ssp_ready, 1)
                if n % 2 == 0:
                    splits(q + 1, q + 6)
                    act.wait_ge(htr_done, NBLK + 1 + n // 2)
                    evac_high(aH, 4, n * BT, C_PLE).then_inc(fh_ready, 1)
                    splits(q + 6, q + CF)
                elif n < NBLK - 1:
                    splits(q + 1, q + CF)
            q += 1

            for n in range(NBLK):
                act.wait_ge(chunk_used, CHUNK_P + n + 1)
                for t in range(NT):
                    ins = fn(pw[:, t, n * NB:(n + 1) * NB], tok_bank(n, t)[:, :], ACT.Copy)
                ins.then_inc(act_evac, 1)
                if n == 0:
                    act.dma_start(gf[:, :], gf_d.partition_broadcast(P)).then_inc(gf_in, 16)
                if n == 1:
                    act.wait_ge(htr_done, NBLK + 3)
                    evac_high(aH, 4, 1 * BT, C_PLE).then_inc(fh_ready, 1)
                if n < NBLK - 1:
                    splits(q, q + 1)
                    q += 1
            act.wait_ge(htr_done, NBLK + 4)
            evac_high(aH, 4, 3 * BT, C_PLE).then_inc(fh_ready, 1)
            splits(q, q + CB)
            q += CB

            act.wait_ge(rp_ready, 1)
            for n in range(NBLK):
                act.wait_ge(chunk_used, CHUNK_E + (n + 1) * CB)
                act.wait_ge(hf_ready, n)
                for t in range(NT):
                    ins = fn(gate[:, t, :], tok_bank(n, t)[:, :], ACT.Sigmoid, scale=rP[:, t:t + 1])
                ins.then_inc(act_evac, 1)
                act.wait_ge(hf_ready, n + 1)
                for t in range(NT):
                    ins = fn(junk[:, t, :], h3[:, t, n * NB:(n + 1) * NB], ACT.Square, accum_out=ssF[:, t, n:n + 1])
                ins.then_inc(ssf_ready, 1)
                hi = min(q + CB, CHUNKS)
                splits(q, hi)
                q = hi

        @block.vector
        def _(dve):
            for first in by_vector:
                dve.sem_inc(first, 1)
            tt, stt, ts = dve.tensor_tensor, dve.scalar_tensor_tensor, dve.tensor_scalar
            order = dve_order

            def split(r, j):
                dve.wait_ge(wh_ready, r * SLOTS + (j + 1))
                tt(wL[:, j, :, :], raw[:, j, :, :], wH[:, j, :, :].bitcast(F32), ALU.subtract).then_inc(wl_ready, 1)

            def splits(lo, hi):
                while lo < hi:
                    if lo % SLOTS == 0 and hi - lo >= 2 * SLOTS:
                        with dve.Fori(lo // SLOTS, hi // SLOTS) as r:
                            for j in range(SLOTS):
                                split(r, j)
                        lo = hi // SLOTS * SLOTS
                    else:
                        split(lo // SLOTS, lo % SLOTS)
                        lo += 1

            def evac_low(dst, high, banks, k0, col):
                for m in range(BT):
                    ins = stt(dst[:, bass.ds(k0 + m, 1), :].rearrange("p a c -> p (a c)"),
                              ps[banks + m // 2][:, (m % 2) * SEQ:(m % 2 + 1) * SEQ],
                              prm[:, bass.ds(k0 + (col + m), 1)],
                              high[:, bass.ds(k0 + m, 1), :].rearrange("p a c -> p (a c)").bitcast(F32),
                              ALU.mult, ALU.subtract)
                return ins

            dve.wait_ge(prm_in, 16)
            for k in range(KD):
                if k % 4 == 0:
                    dve.wait_ge(xT_in[k // 4], 16)
                dve.wait_ge(ah_ready, k + 1)
                stt(aL[:, k, :], xTs[:, k, :], prm[:, C_MIX + k:C_MIX + k + 1], aH[:, k, :].bitcast(F32),
                    ALU.mult, ALU.subtract).then_inc(al_ready, 1)
                if k % 2 == 1:
                    split(k // 2 // SLOTS, k // 2 % SLOTS)
            dve.wait_ge(wdth_ready, 1)
            tt(wdtL[:, :, :], wdtr[:, :, :], wdtH[:, :, :].bitcast(F32), ALU.subtract).then_inc(wdtl_ready, 1)
            splits(2 * SLOTS, AHEAD + (NBLK - 1) * CB)

            dve.wait_ge(dtmm_done, 1)
            dve.wait_ge(r0_ready, 1)
            dve.wait_ge(rows_in, 16)
            for t in range(NT):
                ins = stt(dtu[:, t * HEADS:(t + 1) * HEADS], ps[4 + t][:, 0:HEADS], r0[:, t:t + 1], rows[:, 0, :],
                          ALU.mult, ALU.add)
            ins.then_inc(dtu_ready, 1)
            q = AHEAD + (NBLK - 1) * CB
            splits(q, q + 2)
            dve.wait_ge(dte_ready, 2)
            order.mark(ts(dtq, dte, 2.0, None, ALU.add))
            order.wait(dve)
            order.mark(dve.reciprocal(dtq, dtq))
            order.wait(dve)
            order.mark(tt(dte, dte, dtq, ALU.mult))
            order.wait(dve)
            order.mark(tt(dtq, dte, dte, ALU.mult))
            order.wait(dve)
            terms = 8
            order.mark(ts(acc, dtq, 1.0 / (2 * terms + 1), None, ALU.mult))
            for n in range(terms - 1, 0, -1):
                order.wait(dve)
                order.mark(stt(acc, acc, 1.0 / (2 * n + 1), dtq, ALU.add, ALU.mult))
            order.wait(dve)
            order.mark(stt(acc, acc, 1.0, dte, ALU.add, ALU.mult))
            order.mark(ts(dtu, dtu, 0.0, None, ALU.max))
            order.wait(dve)
            order.mark(stt(dt, acc, 2.0, dtu, ALU.mult, ALU.add))
            order.wait(dve)
            for t in range(NT):
                ins = stt(adt[:, t * HEADS:(t + 1) * HEADS], dt[:, t * HEADS:(t + 1) * HEADS], -1.0, rows[:, 1, :],
                          ALU.mult, ALU.mult)
            ins.then_inc(adt_ready, 1)
            splits(q + 2, q + CB)

            dve.wait_ge(rb_ready, 1)
            dve.wait_ge(pads_ready, 1)
            dve.wait_ge(ea_ready, 1)
            rb2 = rb[:, :].unsqueeze(1).broadcast_to([P, 2, SEQ])
            with dve.Fori(0, GROUPS // 2) as i:
                order.enter(i, 12)
                for b in range(2):
                    g = i * 2 + b

                    def s(c):
                        split(i * 4 + (3 + 2 * G0 + 2 * b + c // 4), c % 4)

                    dve.wait_ge(chunk_used, g * CB + (G0 + 1) * CB)
                    for n in range(2):
                        ins = tt(xs[:, 2 * n:2 * n + 2, 3:3 + SEQ],
                                 ps[2 * b + n][:, :].rearrange("p (m c) -> p m c", m=2), rb2, ALU.mult)
                    ins.then_inc(dve_evac, 1)
                    s(0)
                    dve.wait_ge(cv0_ready, g + 1)
                    for tap in (2, 1, 0):
                        for m in range(BT):
                            ins = stt(cv[:, m, :], xs[:, m, tap:tap + SEQ],
                                      prm[:, bass.ds(g * (5 * BT) + (C_CONV + 5 * m + tap), 1)], cv[:, m, :],
                                      ALU.mult, ALU.add)
                        if tap:
                            order.mark(ins)
                            s(3 - tap)
                            order.wait(dve)
                        else:
                            ins.then_inc(conv_ready, 1)
                    s(3)
                    dve.wait_ge(scores_done, g + 1)
                    dve.tensor_copy(btok[:, :], ps[5][:, 0:P]).then_inc(btok_ready, 1)
                    order.mark(tt(sc[:, :, :], ps[5][:, P:3 * P].rearrange("p (c l) -> p c l", c=NT),
                                  upper[:, :].unsqueeze(1).broadcast_to([P, NT, P]), ALU.mult))
                    s(4)
                    dve.wait_ge(exp_ready, g * 2 + 2)
                    order.wait(dve)
                    for c in range(NT):
                        ins = tt(E[:, c, :, :], E[:, c, :, :], sc[:, c, :].unsqueeze(1).broadcast_to([P, HPG, P]),
                                 ALU.mult)
                    ins.then_inc(m_ready, 1)
                    s(5)
                    s(6)
                    dve.wait_ge(y_done, g + 1 + 1)
                    dve.wait_ge(yx_ready, g + 1 + 1)
                    order.mark(tt(y[:, :, :].rearrange("p t c -> p (t c)"), ps[6][:, :],
                                  yx[:, :, :].rearrange("p t c -> p (t c)"), ALU.add))
                    order.mark(tt(yo[:, :].rearrange("p (h e) -> p h e", h=HPG),
                                  ps[7][:, 0:GC].rearrange("p (h e) -> p h e", h=HPG),
                                  ea[:, bass.ds(g * HPG + HEADS, HPG)].unsqueeze(2).broadcast_to([P, HPG, HD]),
                                  ALU.mult))
                    order.wait(dve)
                    order.mark(tt(y[:, 1, :], y[:, 1, :], yo[:, :], ALU.add))
                    order.wait(dve)
                    tt(y[:, :, :], y[:, :, :], z4[:, bass.ds(g, 1), :, :].rearrange("p g t c -> p (g t) c"),
                       ALU.mult).then_inc(y_ready, 1)
                    s(7)
                    dve.wait_ge(yh_ready, g + 1)
                    for m in range(2):
                        k = bass.ds(g * 2 + m, 1)
                        ins = stt(yBL[:, k, :].rearrange("p a c -> p (a c)"), ps[5][:, m * SEQ:(m + 1) * SEQ],
                                  prm[:, bass.ds(g * 2 + (C_SSM + m), 1)],
                                  yBH[:, k, :].rearrange("p a c -> p (a c)").bitcast(F32), ALU.mult, ALU.subtract)
                    ins.then_inc(yl_ready, 1)
                order.leave(GROUPS // 2)

            with dve.Fori(0, NBLK) as i:
                def s(lo, hi):
                    for c in range(lo, hi):
                        split(i * 4 + (3 + 2 * V0 + c // 4), c % 4)

                order.enter(i, 3)
                s(0, 1)
                dve.wait_ge(act_evac, i * 2 + (A_VU + 1))
                for t in range(NT):
                    for gg in range(BT):
                        ins = dve.bn_stats(bst[:, t * BT + gg, :], v[:, t, gg * P:(gg + 1) * P])
                order.mark(ins)
                order.wait(dve)
                s(1, 2)
                for n in range(NT * BT):
                    ins = dve.bn_aggr(mv[:, n, :], bst[:, n, :])
                ins.then_inc(mv_ready, 1)
                s(2, 3)
                dve.wait_ge(rs_ready, i * 2 + 2)
                for t in range(NT):
                    for gg in range(BT):
                        n = t * BT + gg
                        ins = ts(v[:, t, gg * P:(gg + 1) * P], v[:, t, gg * P:(gg + 1) * P],
                                 rs[:, n:n + 1], nm[:, n:n + 1], ALU.mult, ALU.subtract)
                order.mark(ins)
                s(3, 4)
                dve.wait_ge(ws_in, i * 32 + 32)
                order.wait(dve)
                order.mark(tt(v, v, lnr[:, 0, :].unsqueeze(1).broadcast_to([P, NT, NB]), ALU.mult))
                order.wait(dve)
                tt(v, v, lnr[:, 1, :].unsqueeze(1).broadcast_to([P, NT, NB]), ALU.add).then_inc(vn_ready, 1)
                s(4, CB + 1)
                dve.wait_ge(act_evac, i * 2 + (A_VU + 2))
                dve.wait_ge(sg_done, i + 1 + 1)
                for t in range(NT):
                    for gg in range(BT):
                        ins = stt(u[:, t, gg * P:(gg + 1) * P], ps[4 + t][:, gg * P:(gg + 1) * P],
                                  prm[:, bass.ds(i * BT + (C_BS + gg), 1)], u[:, t, gg * P:(gg + 1) * P],
                                  ALU.add, ALU.mult)
                ins.then_inc(ya_ready, 1)
                s(CB + 1, CB + 6)
                dve.wait_ge(yah_ready, i + 1)
                evac_low(yAL, yAH, 6, i * BT, C_A).then_inc(yal_ready, 1)
                s(CB + 6, 2 * CB)
                order.leave(NBLK)
            dve.wait_ge(ssa_ready, NBLK)
            dve.reduce_sum(sA, ssA, AX.X).then_inc(sa_ready, 1)

            dve.wait_ge(x2_in, 16)
            dve.wait_ge(ra_ready, 1)
            with dve.Fori(0, NBLK) as n:
                def s(lo, hi):
                    for c in range(lo, hi):
                        split(n * 4 + (3 + 2 * O0 + c // 4), c % 4)

                dve.wait_ge(chunk_used, n * (2 * CB) + (O0 + 1) * CB)
                dve.wait_ge(hcopy_done, n + 1)
                dve.wait_ge(ssh_ready, n + 1)
                for t in range(NT):
                    ins = tt(hb[:, t, :], tok_bank(0, t)[:, :], h3[:, t, bass.ds(n * NB, NB)], ALU.add)
                ins.then_inc(dve_evac, 1)
                s(0, CB)
                dve.wait_ge(chunk_used, n * (2 * CB) + (O0 + 2) * CB)
                for t in range(NT):
                    ins = stt(hb[:, t, :], tok_bank(1, t)[:, :], rA[:, t:t + 1], hb[:, t, :], ALU.mult, ALU.add)
                ins.then_inc(dve_evac, 1)
                s(CB, CB + 4)
                dve.wait_ge(fh_ready, n + 1)
                evac_low(aL, aH, 4, n * BT, C_FFN).then_inc(fl_ready, 1)
                s(CB + 4, 2 * CB)
            dve.wait_ge(ssh_ready, NBLK + 1)
            dve.reduce_sum(sH, ssH, AX.X).then_inc(sh_ready, 1)

            dve.wait_ge(rb_ready, 2)
            dve.wait_ge(fpads_ready, 1)
            with dve.Fori(0, FB) as i:
                order.enter(i, 2)
                for b, cf in enumerate((cfG, cfU)):
                    def s(lo, hi):
                        for c in range(lo, hi):
                            split(i * 4 + (3 + 2 * F0 + 2 * b + c // 4), c % 4)

                    dve.wait_ge(chunk_used, i * (2 * CB) + (F0 + 1 + b) * CB)
                    for n in range(2):
                        ins = tt(xf[:, 2 * n:2 * n + 2, 2:2 + SEQ],
                                 ps[2 * b + n][:, :].rearrange("p (m c) -> p m c", m=2), rb2, ALU.mult)
                    ins.then_inc(dve_evac, 1)
                    s(0, 2)
                    dve.wait_ge(fc0_ready, i * 2 + (b + 1))
                    for tap in (1, 0):
                        for m in range(BT):
                            ins = stt(cf[:, m, :], xf[:, m, tap:tap + SEQ],
                                      prm[:, bass.ds(i * (4 * BT) + (C_CONVF + 4 * (m + b * KF) + tap), 1)],
                                      cf[:, m, :], ALU.mult, ALU.add)
                        if tap:
                            order.mark(ins)
                            s(2, 3)
                            order.wait(dve)
                        else:
                            ins.then_inc(fconv_ready, 1)
                    s(3, 4)
                    if b == 0:
                        s(4, 8)
                        continue
                    dve.wait_ge(fsilu_ready, i + 1)
                    dve.wait_ge(fconv_ready, i * 2 + 2)
                    tt(cfU[:, :, :], cfU[:, :, :], cfG[:, :, :], ALU.mult).then_inc(gu_ready, 1)
                    s(4, 6)
                    dve.wait_ge(guh_ready, i + 1)
                    tt(guL[:, bass.ds(i * BT, BT), :], cfU[:, :, :], guH[:, bass.ds(i * BT, BT), :].bitcast(F32),
                       ALU.subtract).then_inc(gul_ready, 1)
                    s(6, 8)
                order.leave(FB)

            q = CHUNK_D + AHEAD
            splits(q, q + 4)
            dve.wait_ge(ph_ready, 1)
            tt(pL[:, :, :], praw, pH[:, :, :].bitcast(F32), ALU.subtract).then_inc(pl_ready, 1)
            splits(q + 4, CHUNK_D + CF + SLOTS)

            for n in range(NBLK):
                q = CHUNK_D + (n + 1) * CF + SLOTS
                dve.wait_ge(chunk_used, CHUNK_D + (n + 1) * CF)
                dve.wait_ge(hcopy_done, NBLK + (n + 1) // 2 + 1)
                for t in range(NT):
                    src = h3[:, t, n * NB:(n + 1) * NB]
                    ins = tt(src if n % 2 else hb[:, t, :], tok_bank(n, t)[:, :], src, ALU.add)
                ins.then_inc(dve_evac, 1)
                splits(q, q + 1)
                if n % 2 == 0:
                    splits(q + 1, q + 7)
                    dve.wait_ge(fh_ready, NBLK + 1 + n // 2)
                    evac_low(aL, aH, 4, n * BT, C_PLE).then_inc(fl_ready, 1)
                    splits(q + 7, q + CF)
                elif n < NBLK - 1:
                    splits(q + 1, q + CF)
            q += 1
            dve.wait_ge(ssp_ready, NBLK)
            dve.reduce_sum(sP, ssP, AX.X).then_inc(sp_ready, 1)
            for n in range(1, NBLK):
                splits(q, q + 1)
                q += 1
                if n == 1:
                    dve.wait_ge(fh_ready, NBLK + 3)
                    evac_low(aL, aH, 4, 1 * BT, C_PLE).then_inc(fl_ready, 1)
            dve.wait_ge(fh_ready, NBLK + 4)
            evac_low(aL, aH, 4, 3 * BT, C_PLE).then_inc(fl_ready, 1)
            splits(q, q + CB)
            q += CB

            for n in range(NBLK):
                blk = slice(n * NB, (n + 1) * NB)
                dve.wait_ge(act_evac, A_E + n + 1)
                order.mark(tt(gate[:, :, :], gate[:, :, :], pw[:, :, blk], ALU.mult))
                order.wait(dve)
                tt(h3[:, :, blk], h3[:, :, blk], gate[:, :, :], ALU.add).then_inc(hf_ready, 1)
                hi = min(q + CB, CHUNKS)
                splits(q, hi)
                q = hi
            dve.wait_ge(ssf_ready, NBLK)
            dve.reduce_sum(sF, ssF, AX.X).then_inc(sf_ready, 1)
            dve.wait_ge(gf_in, 16)
            dve.wait_ge(rf_ready, 1)
            for t in range(NT):
                stt(h3[:, t, :], h3[:, t, :], rF[:, t:t + 1], gf[:, :], ALU.mult, ALU.mult).then_inc(out_ready, 1)

        @block.tensor
        def _(pe):
            for first in by_tensor:
                pe.sem_inc(first, 1)
            mm = pe.matmul

            def tok_chunk(chunk, slot, high, low, k0, blk, first, last):
                pe.wait_ge(wl_ready, chunk + 1)
                for kk in range(KC):
                    for t in range(NT):
                        tok = slice(t * P, (t + 1) * P)
                        for n, (a, w) in enumerate(((high, wH), (high, wL), (low, wH))):
                            ins = mm(tok_bank(blk, t)[:, :], a[:, k0 + kk, tok], w[:, slot, kk, :],
                                     start=first and kk == 0 and n == 0, stop=last and kk == KC - 1 and n == 2)
                ins.then_inc(chunk_used, 1)

            def ch_chunk(chunk, slot, k0, blk, first, last):
                pe.wait_ge(wl_ready, chunk + 1)
                for kk in range(KC):
                    for m in range(BT):
                        out_m = ps[2 * (blk % 2) + m // 2][:, (m % 2) * SEQ:(m % 2 + 1) * SEQ]
                        for n, (w, a) in enumerate(((wH, aH), (wH, aL), (wL, aH))):
                            ins = mm(out_m, w[:, slot, kk, m * P:(m + 1) * P], a[:, k0 + kk, :],
                                     start=first and kk == 0 and n == 0 and m % 2 == 0,
                                     stop=last and kk == KC - 1 and n == 2, skip_group_check=True)
                ins.then_inc(chunk_used, 1)

            def transposes(src, banks):
                for m in range(BT):
                    for t in range(NT):
                        ins = pe.transpose(ps[banks + m // 2][:, (m % 2) * SEQ + t * P:(m % 2) * SEQ + (t + 1) * P],
                                           src[:, t, m * P:(m + 1) * P], ident[:, :])
                return ins

            def spread(n):
                pe.wait_ge(dg_ready, n * NT)
                mm(ps[6][:, 0:SEQ], ones[:, :], dg[:, :, :].rearrange("p t c -> p (t c)"), start=True,
                   stop=True).then_inc(rbmm_done, 1)

            def ssd_decays(g):
                pe.wait_ge(y_ready, g + 1)
                for c in range(NT):
                    pe.wait_ge(ld_ready, g * 2 + (c + 1))
                    for hh in range(HPG):
                        ins = mm(ps[6 + c][:, hh * P:(hh + 1) * P], ld[:, c, hh, :], upper[:, :], start=True, stop=True)
                    ins.then_inc(diff_done, 1)

            def ssd_scores(g):
                pe.wait_ge(silu_ready, g + 1)
                pe.wait_ge(st_ready, g + 1)
                pe.wait_ge(yl_ready, g + 1)
                for t in range(NT):
                    pe.transpose(ps[4][:, t * GC:t * GC + P], cv[:, 0, t * P:(t + 1) * P], ident[:, :])
                    ins = pe.transpose(ps[4][:, t * GC + P:(t + 1) * GC], cv[:, 1, t * P:(t + 1) * P], ident[:, :])
                ins.then_inc(xtr_done, 1)
                pe.transpose(ps[5][:, 0:P], cv[:, 2, 0:P], ident[:, :])
                for c in range(NT):
                    chunk = slice(c * P, (c + 1) * P)
                    ins = mm(ps[5][:, (c + 1) * P:(c + 2) * P], cv[:, 2, chunk], cv[:, 3, chunk], start=True, stop=True)
                ins.then_inc(scores_done, 1)

            def ssd_states(g):
                pe.wait_ge(btok_ready, g + 1)
                pe.wait_ge(xd_ready, g + 1)
                mm(ps[4][:, 0:GC], btok[:, :], xdd[:, :], start=True, stop=True).then_inc(st_done, 1)

            def ssd_outputs(g):
                pe.wait_ge(m_ready, g + 1)
                pe.wait_ge(st_ready, g + 1 + 1)
                for c in range(NT):
                    for hh in range(HPG):
                        mm(ps[6][:, c * GC + hh * HD:c * GC + (hh + 1) * HD], E[:, c, hh, :],
                           xdt[:, c, hh * HD:(hh + 1) * HD], start=True, stop=True)
                mm(ps[7][:, 0:GC], cv[:, 3, P:2 * P], stT[:, :], start=True, stop=True).then_inc(y_done, 1)

            def ssd_transposes(g):
                pe.wait_ge(yn_ready, g + 1)
                for m in range(2):
                    for t in range(NT):
                        ins = pe.transpose(ps[5][:, m * SEQ + t * P:m * SEQ + (t + 1) * P], y[:, t, m * P:(m + 1) * P],
                                           ident[:, :])
                ins.then_inc(ytr_done, 1)

            for b in range(NBLK):
                if b >= 2:
                    pe.wait_ge(act_evac, A_Z + b - 1)
                for c in range(CB):
                    if b == 0:
                        pe.wait_ge(al_ready, 2 * c + 2)
                    tok_chunk(b * CB + c, c % SLOTS, aH, aL, KC * c, b, c == 0, c == CB - 1)
            pe.wait_ge(wdtl_ready, 1)
            for t in range(NT):
                tok = slice(t * P, (t + 1) * P)
                for k in range(KD):
                    for n, (a, w) in enumerate(((aH, wdtH), (aH, wdtL), (aL, wdtH))):
                        ins = mm(ps[4 + t][:, 0:HEADS], a[:, k, tok], w[:, k, :], start=k == 0 and n == 0,
                                 stop=k == KD - 1 and n == 2)
            ins.then_inc(dtmm_done, 1)
            spread(1)
            pe.wait_ge(act_evac, A_Z + 3)
            for c in range(CB):
                ch_chunk(G0 * CB + c, c % SLOTS, KC * c, G0, c == 0, c == CB - 1)
                if c == 5:
                    pe.wait_ge(adt_ready, 1)
                    mm(ps[7][:, 0:NT * HEADS], upper[:, :], adt, start=True, stop=True)
                    mm(ps[7][:, P:P + HEADS], lower[:, :], adt[:, 0:HEADS], start=True, stop=True)\
                        .then_inc(csmm_done, 1)

            def with_ssd(g, block_chunk):
                for c in range(CB):
                    block_chunk(c)
                    if c == 0:
                        ssd_decays(g)
                    if c == 3:
                        ssd_scores(g)
                    if c == 4:
                        ssd_states(g)
                    if c == 6:
                        ssd_outputs(g)
                    if c == 7:
                        ssd_transposes(g)

            def g_block(g, blk):
                with_ssd(g, lambda c: ch_chunk(g * CB + ((G0 + 1) * CB + c), c % SLOTS, KC * c, blk, c == 0,
                                               c == CB - 1))

            pe.wait_ge(act_evac, A_Z + 4)
            with pe.Fori(0, (GROUPS - 2) // 2) as i:
                for b in range(2):
                    pe.wait_ge(dve_evac, i * 2 + b + 1)
                    g_block(i * 2 + b, b + 1)
            pe.wait_ge(dve_evac, V_G + GROUPS - 2 + 1)
            g_block(GROUPS - 2, GROUPS - 1)

            def vu_block(i, b, side):
                for c in range(CB):
                    tok_chunk(i * (2 * CB) + ((V0 + b) * CB + c), c % SLOTS, aH, aL, KC * c, b, c == 0, c == CB - 1)
                    side(c)

            def spatial(i):
                pe.wait_ge(vn_ready, i + 1)
                pe.wait_ge(ws_ready, i + 1)
                for t in range(NT):
                    for gg in range(BT):
                        ins = mm(ps[4 + t][:, gg * P:(gg + 1) * P], wsT[:, gg, :], v[:, t, gg * P:(gg + 1) * P],
                                 start=True, stop=True)
                ins.then_inc(sg_done, 1)

            def ya_transposes(i):
                pe.wait_ge(ya_ready, i + 1)
                pe.wait_ge(yal_ready, i + 1)
                transposes(u, 6).then_inc(yatr_done, 1)

            pe.wait_ge(dve_evac, V_G + GROUPS - 1 + 1)
            with_ssd(GROUPS - 1, lambda c: tok_chunk(V0 * CB + c, c % SLOTS, aH, aL, KC * c, V0, c == 0, c == CB - 1))
            pe.wait_ge(dve_evac, V_G + GROUPS + 1)
            pe.wait_ge(yl_ready, GROUPS + 1)
            with pe.Fori(0, NBLK - 1) as i:
                pe.wait_ge(act_evac, i * 2 + A_VU)
                vu_block(i, 1, lambda c: spatial(i) if c == 6 else None)
                pe.wait_ge(act_evac, i * 2 + (A_VU + 1))
                vu_block(i + 1, 0, lambda c: ya_transposes(i) if c == 4 else None)
            pe.wait_ge(act_evac, A_VU + 2 * NBLK - 2)
            vu_block(NBLK - 1, 1, lambda c: spatial(NBLK - 1) if c == 6 else None)

            def o_block(n, b, side):
                for c in range(CB):
                    tok_chunk(n * (2 * CB) + ((O0 + b) * CB + c), c % SLOTS, (yBH, yAH)[b], (yBL, yAL)[b], KC * c, b,
                              c == 0, c == CB - 1)
                    side(c)

            def h_transposes(n):
                pe.wait_ge(dve_evac, n * 2 + (V_O + 2) + 1)
                pe.wait_ge(fl_ready, n + 1)
                transposes(hb, 4).then_inc(htr_done, 1)

            pe.wait_ge(act_evac, A_VU + 2 * NBLK - 1)
            o_block(0, 0, lambda c: ya_transposes(NBLK - 1) if c == 4 else None)
            pe.wait_ge(act_evac, A_VU + 2 * NBLK)
            pe.wait_ge(yal_ready, NBLK + 1)
            o_block(0, 1, lambda c: None)
            with pe.Fori(1, NBLK) as n:
                pe.wait_ge(dve_evac, n * 2 + (V_O - 1) + 1)
                o_block(n, 0, lambda c: h_transposes(n - 1) if c == 2 else None)
                pe.wait_ge(dve_evac, n * 2 + V_O + 1)
                o_block(n, 1, lambda c: None)

            def f_block(i, b, side):
                for c in range(CB):
                    ch_chunk(i * (2 * CB) + ((F0 + b) * CB + c), c % SLOTS, KC * c, b, c == 0, c == CB - 1)
                    side(c)

            def first_side(c):
                if c == 2:
                    h_transposes(NBLK - 1)
                if c == 5:
                    pe.wait_ge(fl_ready, NBLK + 1)

            pe.wait_ge(dve_evac, V_O + 2 * NBLK - 1 + 1)
            pe.wait_ge(fl_ready, NBLK - 1 + 1)
            f_block(0, 0, first_side)
            pe.wait_ge(dve_evac, V_O + 2 * NBLK + 1)
            f_block(0, 1, lambda c: spread(2) if c == 1 else None)
            with pe.Fori(1, FB) as i:
                pe.wait_ge(dve_evac, i * 2 + (V_F - 1) + 1)
                f_block(i, 0, lambda c: None)
                pe.wait_ge(dve_evac, i * 2 + V_F + 1)
                f_block(i, 1, lambda c: None)

            with pe.Fori(0, NBLK // 2) as i:
                for b in range(2):
                    pe.wait_ge(dve_evac, i * 2 + (V_D - 1 + b) + 1)
                    for c in range(CF):
                        if KC * c % BT == 0:
                            pe.wait_ge(gul_ready, KC * c // BT + 1 + 1)
                        q = CHUNK_D + b * CF + c
                        tok_chunk(i * (2 * CF) + q, q % SLOTS, guH, guL, KC * c, b, c == 0, c == CF - 1)
                        if b == 1 and c == 4:
                            pe.wait_ge(dve_evac, i * 2 + (V_D + 1) + 1)
                            pe.wait_ge(fl_ready, i + NBLK + 1)
                            transposes(hb, 4).then_inc(htr_done, 1)

            def late_transposes(n, before):
                pe.wait_ge(dve_evac, V_D + n + 1 + 1)
                pe.wait_ge(fl_ready, before + 1)
                transposes(h3[:, :, n * NB:(n + 1) * NB], 4).then_inc(htr_done, 1)

            pe.wait_ge(pl_ready, 1)
            for n in range(NBLK):
                pe.wait_ge(dve_evac, V_D + NBLK - 1 + min(n, 1) + 1)
                if n >= 2:
                    pe.wait_ge(act_evac, A_P + n - 1)
                q = CHUNK_P + n
                tok_chunk(q, q % SLOTS, pH, pL, 0, n, True, True)
                if n == 0:
                    late_transposes(1, NBLK + 2)
            late_transposes(3, NBLK + 3)

            def e_block(q, n, first):
                for c in range(CB):
                    if first and c == 6:
                        pe.wait_ge(fl_ready, NBLK + 4 + 1)
                    tok_chunk(q + c, c % SLOTS, aH, aL, KC * c, n, c == 0, c == CB - 1)

            pe.wait_ge(fl_ready, NBLK + 3 + 1)
            for n in range(NBLK):
                pe.wait_ge(act_evac, A_P + 3 + n)
                e_block(CHUNK_E + n * CB, n, n == 0)


def blocks_of(np, w, chunk_rows):
    k, n = w.shape
    w = w.reshape(k // chunk_rows, KC, P, n // NB, NB)
    return w.transpose(3, 0, 2, 1, 4).reshape(n // NB, k // chunk_rows, P, KC * NB)


def kernel(**inputs):
    import numpy as np
    import concourse.bacc as bacc
    from concourse.bass_utils import run_bass_kernel_spmd

    a = {k: np.asarray(v) for k, v in inputs.items()}
    w_in = a["w_in"][0]
    da = 2 * D
    o_x, o_b, o_c, o_dt = da + D, da + 2 * D, da + 2 * D + GROUPS * P, da + 2 * D + 2 * GROUPS * P

    def cut(w):
        return blocks_of(np, w, KC * P)

    groups = np.concatenate([
        np.concatenate([w_in[:, o_x + g * GC:o_x + (g + 1) * GC], w_in[:, o_b + g * P:o_b + (g + 1) * P],
                        w_in[:, o_c + g * P:o_c + (g + 1) * P]], axis=1) for g in range(GROUPS)], axis=1)

    def pairs(first, second):
        return np.stack([cut(first), cut(second)], axis=1).reshape(-1, P, KC * NB)

    w_out, w_up = a["w_out"][0], a["w_up"][0]
    flat = lambda w: w.reshape(-1, P, KC * NB)
    stream = np.concatenate([
        flat(cut(w_in[:, da:da + D])), flat(cut(groups)), pairs(w_in[:, D:da], w_in[:, :D]),
        pairs(w_out[D:], w_out[:D]), pairs(w_up[:, :D_FF], w_up[:, D_FF:]), flat(cut(a["w_down"][0])),
        flat(cut(a["w_ple"][0])), flat(cut(a["w_ple_gate"][0]))])

    tiles = lambda vec: vec.reshape(-1, P).T
    conv = np.concatenate([a["conv_ssm_w"][0], a["conv_ssm_b"]])
    nbc = GROUPS * P
    conv = np.concatenate([
        conv[:, :D].reshape(5, GROUPS, 2, P), conv[:, D:D + nbc].reshape(5, GROUPS, 1, P),
        conv[:, D + nbc:].reshape(5, GROUPS, 1, P)], axis=2)
    convf = np.concatenate([a["conv_ffn_w"][0], a["conv_ffn_b"]]).reshape(4, 2 * KF, P)
    prm = np.concatenate([
        tiles(a["norm_mix_g"][0]), tiles(a["norm_ffn_g"][0]), tiles(a["norm_ple_g"][0]), tiles(a["norm_a_g"][0]),
        tiles(a["ssm_norm_g"][0]), a["b_s"][0].T, conv.transpose(3, 1, 2, 0).reshape(P, -1),
        convf.transpose(2, 1, 0).reshape(P, -1)], axis=1)
    arrays = {
        "x": a["x"][0],
        "xT": a["x"][0].T.reshape(KD, P, SEQ).transpose(1, 0, 2),
        "wstream": stream.reshape(CHUNKS, P, KC, NB),
        "wdt": w_in[:, o_dt:].reshape(KD, P, HEADS).transpose(1, 0, 2),
        "prm": prm,
        "rows": np.stack([a["dt_bias"][0], a["a_log"][0], a["d_skip"][0]]),
        "wsT": a["w_s"][0].reshape(NBLK, BT, P, P).transpose(0, 3, 1, 2),
        "ln": np.stack([a["ln_a_g"][0].reshape(NBLK, NB), a["ln_a_b"][0].reshape(NBLK, NB)], axis=1),
        "pT": a["p"][0, 0].T.reshape(KC, P, SEQ).transpose(1, 0, 2),
        "gf": a["norm_final_g"],
    }
    nc = bacc.Bacc("TRN2", target_bir_lowering=False, num_devices=1)
    arrays = {"in_" + k: np.ascontiguousarray(v) for k, v in arrays.items()}
    args = [nc.dram_tensor(k, v.shape, F32, kind="ExternalInput").ap() for k, v in arrays.items()]
    out = nc.dram_tensor("out", (SEQ, D), F32, kind="ExternalOutput").ap()
    build(nc, *args, out)
    got = run_bass_kernel_spmd(nc, [arrays], core_ids=[0]).results[0]["out"]
    return got.reshape(1, SEQ, D)
```

```python
from contextlib import ExitStack

import concourse.bass as bass
from concourse import mybir

F32 = mybir.dt.float32
F32R = mybir.dt.float32r
ALU = mybir.AluOpType
ACT = mybir.ActivationFunctionType
AX = mybir.AxisListType

P = 128
SEQ = 256
NT = SEQ // P
D = 2048
KD = D // P
NB = 512
NBLK = D // NB
BT = NB // P
GROUPS = 8
HPG = 4
HD = 64
GC = HPG * HD
HEADS = GROUPS * HPG
D_FF = 5632
KF = D_FF // P
FB = D_FF // NB
D_PLE = 256
EPS = 1e-6

KC = 2
SLOTS = 4
XT_CUTS = (0, 2, 4, 8, 12)
CB = KD // KC
CF = KF // KC

Z0 = 0
G0 = Z0 + NBLK
V0 = G0 + GROUPS
O0 = V0 + 2 * NBLK
F0 = O0 + 2 * NBLK
CHUNK_D = (F0 + 2 * FB) * CB
CHUNK_P = CHUNK_D + NBLK * CF
CHUNK_E = CHUNK_P + NBLK
CHUNKS = CHUNK_E + NBLK * CB
WARM = 16
AHEAD = 12

A_Z, A_VU, A_P, A_E = 0, 4, 12, 16
V_G, V_O, V_F, V_D = 0, 8, 16, 38

C_MIX, C_FFN, C_PLE, C_A, C_SSM, C_BS = 0, 16, 32, 48, 64, 80
C_CONV = 96
C_CONVF = C_CONV + GROUPS * BT * 5
N_PRM = C_CONVF + 2 * KF * 4


class Order:

    def __init__(self, sem):
        self.sem, self.n, self.i, self.per = sem, 0, 0, 0

    def mark(self, instruction):
        instruction.then_inc(self.sem, 1)
        self.n += 1

    def wait(self, engine):
        engine.wait_ge(self.sem, self.per * self.i + self.n)

    def enter(self, i, per, first=0):
        self.i, self.per, self.first, self.start = i, per, first, self.n
        self.n -= per * first

    def leave(self, times):
        self.n += self.per * self.first
        assert self.n - self.start == self.per, (self.n - self.start, self.per)
        self.n, self.i, self.per = self.start + self.per * times, 0, 0


def build(nc, x, xT, wstream, wdt, prm_d, rows_d, wsT_d, ln_d, pT_d, gf_d, out):
    ctx = ExitStack()
    with ctx:
        def sb(stack, name, shape, dt=F32):
            return stack.enter_context(nc.sbuf_tensor(name, shape, dt))

        def sem(name):
            return ctx.enter_context(nc.semaphore(name))

        h = sb(ctx, "h", [P, NT * D])
        h3 = h[:, :].rearrange("p (t d) -> p t d", t=NT)
        aH = sb(ctx, "aH", [P, KD, SEQ], F32R)
        aL = sb(ctx, "aL", [P, KD, SEQ], F32R)
        raw = sb(ctx, "raw", [P, SLOTS, KC, NB])
        wH = sb(ctx, "wH", [P, SLOTS, KC, NB], F32R)
        wL = sb(ctx, "wL", [P, SLOTS, KC, NB], F32R)
        prm = sb(ctx, "prm", [P, N_PRM])
        ident = sb(ctx, "ident", [P, P])
        ones = sb(ctx, "ones", [P, P])
        rb = sb(ctx, "rb", [P, SEQ])
        dg = sb(ctx, "dg", [P, NT, P])
        small = sb(ctx, "small", [P, 512])
        at = [0]

        def cols(n, *shape):
            v = small[:, at[0]:at[0] + n]
            at[0] += n
            assert at[0] <= 512
            if len(shape) == 2:
                v = v.rearrange("p (a b) -> p a b", b=shape[1])
            return v

        half, eps, inv_d, inv_g = (cols(8) for _ in range(4))
        ss0, r0 = cols(2), cols(2)
        ssA, sA, rA = cols(8, NT, NBLK), cols(2), cols(2)
        ssH, sH, rH = cols(8, NT, NBLK), cols(2), cols(2)
        ssP, sP, rP = cols(8, NT, NBLK), cols(2), cols(2)
        ssF, sF, rF = cols(8, NT, NBLK), cols(2), cols(2)
        ssG, rG = cols(2), cols(2)
        mv, rs, nm = cols(16, 8, 2), cols(8), cols(8)
        bst = cols(48, 8, 6)

        sqa = h[:, 0:1024].rearrange("p (k t) -> p k t", k=BT)
        sqs = h[:, 1024:2048].rearrange("p (k t) -> p k t", k=BT)
        z4 = h[:, :].rearrange("p (g t c) -> p g t c", g=GROUPS, t=NT)
        v = h[:, 0:1024].rearrange("p (t c) -> p t c", t=NT)
        u = h[:, 1024:2048].rearrange("p (t c) -> p t c", t=NT)
        wsT = h[:, 2048:2560].rearrange("p (g t) -> p g t", g=BT)
        lnr = h[:, 2560:3584].rearrange("p (a c) -> p a c", a=2)

        mix = ExitStack()
        yBH = sb(mix, "yBH", [P, KD, SEQ], F32R)
        yBL = sb(mix, "yBL", [P, KD, SEQ], F32R)
        yAH = sb(mix, "yAH", [P, KD, SEQ], F32R)
        yAL = sb(mix, "yAL", [P, KD, SEQ], F32R)
        upper = sb(mix, "upper", [P, P])
        lower = sb(mix, "lower", [P, P])
        lowerR = sb(mix, "lowerR", [P, P], F32R)
        rows = sb(mix, "rows", [P, 3, HEADS])
        dts = sb(mix, "dts", [P, 8, NT * HEADS])
        dt, adt, ea, acc, sq_, dtu, dte, dtq = (dts[:, n, :] for n in range(8))
        adtH = sb(mix, "adtH", [P, NT * HEADS], F32R)
        adtL = sb(mix, "adtL", [P, NT * HEADS], F32R)
        ed = sb(mix, "ed", [P, HEADS])
        start = ExitStack()
        xTs = sb(start, "xTs", [P, KD, SEQ])
        wdtr = sb(start, "wdtr", [P, KD, HEADS])
        wdtH = sb(start, "wdtH", [P, KD, P], F32R)
        wdtL = sb(start, "wdtL", [P, KD, P], F32R)
        dtT = sb(start, "dtT", [P, SEQ])
        start.close()
        xs = sb(mix, "xs", [P, BT, 3 + SEQ])
        cv = sb(mix, "cv", [P, BT, SEQ])
        xtok = sb(mix, "xtok", [P, NT, GC])
        btok = sb(mix, "btok", [P, P])
        ct = sb(mix, "ct", [P, P])
        xdt = sb(mix, "xdt", [P, NT, GC])
        xdd = sb(mix, "xdd", [P, GC])
        uaH = sb(mix, "uaH", [P, NT, HPG, P], F32R)
        uaL = sb(mix, "uaL", [P, NT, HPG, P], F32R)
        sc = sb(mix, "sc", [P, NT, P])
        E = sb(mix, "E", [P, NT, HPG, P])
        stT = sb(mix, "stT", [P, GC])
        yx = sb(mix, "yx", [P, NT, GC])
        y = sb(mix, "y", [P, NT, GC])
        yo = sb(mix, "yo", [P, GC])
        mix.close()

        ffn = ExitStack()
        guH = sb(ffn, "guH", [P, KF, SEQ], F32R)
        guL = sb(ffn, "guL", [P, KF, SEQ], F32R)
        xf = sb(ffn, "xf", [P, BT, 2 + SEQ])
        cfG = sb(ffn, "cfG", [P, BT, SEQ])
        cfU = sb(ffn, "cfU", [P, BT, SEQ])
        pH = sb(ffn, "pH", [P, KC, SEQ], F32R)
        pL = sb(ffn, "pL", [P, KC, SEQ], F32R)
        hb = cfU[:, :, :].rearrange("p (t a) c -> p t (a c)", t=NT)
        junk = cfG[:, :, :].rearrange("p (t a) c -> p t (a c)", t=NT)
        praw = xf[:, 0:KC, 2:2 + SEQ]
        ffn.close()
        last = ExitStack()
        pw = sb(last, "pw", [P, NT, D])
        gate = sb(last, "gate", [P, NT, NB])
        gf = sb(last, "gf", [P, D])
        last.close()

        ps = [ctx.enter_context(nc.psum_tensor(f"ps{n}", [P, NB], F32)) for n in range(8)]

        def tok_bank(block, t):
            return ps[2 * (block % 2) + t]

        raw_in = [sem(f"raw_in{j}") for j in range(SLOTS)]
        wh_ready, wl_ready, chunk_used = sem("wh_ready"), sem("wl_ready"), sem("chunk_used")
        act_evac, dve_evac = sem("act_evac"), sem("dve_evac")
        xT_in = [sem(f"xT_in{j}") for j in range(len(XT_CUTS))]
        gain_in, prm_in, rows_in, wdt_in = (sem(n) for n in ("gain_in", "prm_in", "rows_in", "wdt_in"))
        sq_ready, ssmm_done = sem("sq_ready"), sem("ssmm_done")
        x2_in = [sem(f"x2_in{pair}") for pair in range(2)]
        const_ready, masks_ready, warm_ready = sem("const_ready"), sem("masks_ready"), sem("warm_ready")
        ah_ready, al_ready = sem("ah_ready"), sem("al_ready")
        ss0_ready, r0_ready, dg_ready, rbmm_done, rb_ready = (
            sem(n) for n in ("ss0_ready", "r0_ready", "dg_ready", "rbmm_done", "rb_ready"))
        wdth_ready, wdtl_ready, dtmm_done, csmm_done = (
            sem(n) for n in ("wdth_ready", "wdtl_ready", "dtmm_done", "csmm_done"))
        wpad_ready, dtt_ready, dtu_ready, dte_ready, adt_ready, ea_ready = (
            sem(n) for n in ("wpad_ready", "dtt_ready", "dtu_ready", "dte_ready", "adt_ready", "ea_ready"))
        dttr_done = sem("dttr_done")
        cv0_ready, conv_ready, silu_ready = sem("cv0_ready"), sem("conv_ready"), sem("silu_ready")
        ua_ready, diff_done, exp_ready = sem("ua_ready"), sem("diff_done"), sem("exp_ready")
        xtr_done, scores_done, tok_ready = sem("xtr_done"), sem("scores_done"), sem("tok_ready")
        btok_ready, ct_ready = sem("btok_ready"), sem("ct_ready")
        xd_ready, yx_ready, st_done, st_ready = sem("xd_ready"), sem("yx_ready"), sem("st_done"), sem("st_ready")
        m_ready, y_done, y_ready = sem("m_ready"), sem("y_done"), sem("y_ready")
        ssg_ready, rg_ready, yn_ready = sem("ssg_ready"), sem("rg_ready"), sem("yn_ready")
        ytr_done, yh_ready, yl_ready = sem("ytr_done"), sem("yh_ready"), sem("yl_ready")
        ws_in, ws_ready, mv_ready, rs_ready, vn_ready = (
            sem(n) for n in ("ws_in", "ws_ready", "mv_ready", "rs_ready", "vn_ready"))
        sg_done, ya_ready, ssa_ready, yatr_done, yah_ready, yal_ready = (
            sem(n) for n in ("sg_done", "ya_ready", "ssa_ready", "yatr_done", "yah_ready", "yal_ready"))
        sa_ready, ra_ready = sem("sa_ready"), sem("ra_ready")
        hcopy_done, ssh_ready, htr_done, fh_ready, fl_ready = (
            sem(n) for n in ("hcopy_done", "ssh_ready", "htr_done", "fh_ready", "fl_ready"))
        sh_ready, rh_ready = sem("sh_ready"), sem("rh_ready")
        pads_ready, fpads_ready = sem("pads_ready"), sem("fpads_ready")
        fc0_ready, fconv_ready, fsilu_ready, gu_ready, guh_ready, gul_ready = (
            sem(n) for n in ("fc0_ready", "fconv_ready", "fsilu_ready", "gu_ready", "guh_ready", "gul_ready"))
        p_in, ph_ready, pl_ready, gf_in = sem("p_in"), sem("ph_ready"), sem("pl_ready"), sem("gf_in")
        ssp_ready, sp_ready, rp_ready = sem("ssp_ready"), sem("sp_ready"), sem("rp_ready")
        e0_done, hf_ready, hg_ready, ssf_ready, sf_ready, rf_ready, out0_ready, out1_ready, stored = (
            sem(n) for n in ("e0_done", "hf_ready", "hg_ready", "ssf_ready", "sf_ready", "rf_ready", "out0_ready",
                             "out1_ready", "stored"))
        by_tensor = (y_done, sg_done, diff_done)
        by_vector = (y_ready, yl_ready, gul_ready, yal_ready, fl_ready, dve_evac)
        by_scalar = (st_ready, ssh_ready)
        by_gpsimd = (yx_ready, hcopy_done)
        act_order, dve_order, pool_order = Order(sem("act_order")), Order(sem("dve_order")), Order(sem("pool_order"))

        block = ctx.enter_context(nc.Block())

        @block.sync
        def _(sp):
            sp.dma_start(prm[:, 0:C_CONV], prm_d[:, 0:C_CONV]).then_inc(gain_in, 16)
            for j, (k0, k1) in enumerate(zip(XT_CUTS, XT_CUTS[1:] + (KD,))):
                sp.dma_start(xTs[:, k0:k1, :], xT[:, k0:k1, :]).then_inc(xT_in[j], 16)
                if j < SLOTS:
                    sp.dma_start(raw[:, j, :, :], wstream[j]).then_inc(raw_in[j], 16)
            sp.dma_start(wdtr[:, :, :], wdt).then_inc(wdt_in, 16)

            def refill(r, j):
                sp.wait_ge(wl_ready, r * SLOTS + (j + 1 - SLOTS))
                sp.dma_start(raw[:, j, :, :], wstream[r * SLOTS + j]).then_inc(raw_in[j], 16)

            for j in range(SLOTS):
                refill(1, j)
            sp.dma_start(rows[:, :, :], rows_d.partition_broadcast(P)).then_inc(rows_in, 16)
            sp.dma_start(prm[:, C_CONV:N_PRM], prm_d[:, C_CONV:N_PRM]).then_inc(prm_in, 16)
            with sp.Fori(2, CHUNKS // SLOTS) as r:
                for j in range(SLOTS):
                    refill(r, j)
            for half in range(2):
                blk = slice(half * D // 2, (half + 1) * D // 2)
                for t, final in enumerate((out0_ready, out1_ready)):
                    sp.wait_ge(final, half + 1)
                    sp.dma_start(out[t * P:(t + 1) * P, blk], pw[:, t, blk]).then_inc(stored, 16)
            sp.wait_ge(stored, 16 * 2 * NT)

        @block.gpsimd
        def _(pool):
            for first in by_gpsimd:
                pool.sem_inc(first, 1)
            tt = pool.tensor_tensor
            order = pool_order

            def rsqrt(dst, src, inverse, done):
                order.mark(tt(dst, src, inverse[:, 0:NT], ALU.mult))
                order.wait(pool)
                order.mark(tt(dst, dst, eps[:, 0:NT], ALU.add))
                order.wait(pool)
                tt(dst, dst, half[:, 0:NT], ALU.pow).then_inc(done, 1)

            pool.memset(eps, EPS).then_inc(const_ready, 1)
            pool.memset(inv_d, 1.0 / D).then_inc(const_ready, 1)
            pool.memset(inv_g, 1.0 / GC).then_inc(const_ready, 1)
            pool.memset(half, -0.5).then_inc(const_ready, 1)
            pool.memset(ones[:, :], 1.0).then_inc(const_ready, 1)
            pool.memset(ident[:, :], 0.0).then_inc(const_ready, 1)
            pool.wait_ge(const_ready, 6)
            pool.affine_select(out=ident[:, :], in_=ident[:, :], compare_op=ALU.not_equal, fill=1.0, base=0,
                               pattern=[[-1, P]], channel_multiplier=1).then_inc(const_ready, 1)
            pool.affine_select(out=upper[:, :], in_=ones[:, :], compare_op=ALU.is_ge, fill=0.0, base=0,
                               pattern=[[1, P]], channel_multiplier=-1).then_inc(masks_ready, 1)
            pool.affine_select(out=lower[:, :], in_=ones[:, :], compare_op=ALU.is_ge, fill=0.0, base=-1,
                               pattern=[[-1, P]], channel_multiplier=1).then_inc(masks_ready, 1)
            pool.wait_ge(masks_ready, 2)
            pool.tensor_copy(lowerR[:, :], lower[:, :]).then_inc(masks_ready, 1)
            for part in (wdtH, wdtL):
                pool.memset(part[:, :, HEADS:P].bitcast(F32), 0.0).then_inc(wpad_ready, 1)
            pool.wait_ge(xT_in[0], 16)
            for k in range(0, KD, BT):
                pool.wait_ge(xT_in[1 + k // BT], 16)
                order.mark(tt(sqs if k else sqa, xTs[:, k:k + BT, :], xTs[:, k:k + BT, :], ALU.mult))
                order.wait(pool)
                if k:
                    order.mark(tt(sqa, sqa, sqs, ALU.add))
                    order.wait(pool)
            order.mark(tt(sqa[:, 0:2, :], sqa[:, 0:2, :], sqa[:, 2:4, :], ALU.add))
            order.wait(pool)
            tt(sqa[:, 0, :], sqa[:, 0, :], sqa[:, 1, :], ALU.add).then_inc(sq_ready, 1)
            pool.wait_ge(ss0_ready, 1)
            rsqrt(r0, ss0, inv_d, r0_ready)
            pool.wait_ge(r0_ready, 1)
            pool.wait_ge(const_ready, 7)
            pool.wait_ge(warm_ready, 1)
            for t in range(NT):
                pool.tensor_scalar(dg[:, t, :], ident[:, :], r0[:, t:t + 1], None, ALU.mult).then_inc(dg_ready, 1)
            pool.wait_ge(dttr_done, 1)
            pool.memset(xs[:, :, 0:3], 0.0).then_inc(pads_ready, 1)
            pool.wait_ge(adt_ready, 2)
            pool.wait_ge(ea_ready, 1)

            def ln_factors(i):
                pool.wait_ge(ws_in, i * 32 + 32)
                pool.wait_ge(mv_ready, i + 1)
                order.mark(tt(rs, mv[:, :, 1], eps, ALU.add))
                order.wait(pool)
                tt(rs, rs, half, ALU.pow).then_inc(rs_ready, 1)
                pool.wait_ge(rs_ready, i * 2 + 1)
                tt(nm, mv[:, :, 0], rs, ALU.mult).then_inc(rs_ready, 1)
                pool.affine_select(out=wsT, in_=wsT, compare_op=ALU.is_ge, fill=0.0, base=0,
                                   pattern=[[0, BT], [1, P]], channel_multiplier=-1).then_inc(ws_ready, 1)

            def window(g, one, two):
                if two:
                    pool.wait_ge(tok_ready, g)
                    pool.wait_ge(y_done, g)
                    for c in range(NT):
                        d_c = dt[:, bass.ds(g * HPG + (c * HEADS - HPG), HPG)].unsqueeze(2)\
                            .broadcast_to([P, HPG, HD])
                        ins = tt(xdt[:, c, :].rearrange("p (h e) -> p h e", h=HPG),
                                 xtok[:, c, :].rearrange("p (h e) -> p h e", h=HPG), d_c, ALU.mult)
                        if c == 0:
                            order.mark(ins)
                    order.wait(pool)
                    tt(xdd[:, :].rearrange("p (h e) -> p h e", h=HPG),
                       xdt[:, 0, :].rearrange("p (h e) -> p h e", h=HPG),
                       ed[:, bass.ds(g * HPG - HPG, HPG)].unsqueeze(2).broadcast_to([P, HPG, HD]),
                       ALU.mult).then_inc(xd_ready, 1)
                    pool.wait_ge(y_ready, g)
                    skip = rows[:, 2, bass.ds(g * HPG - HPG, HPG)].unsqueeze(2).broadcast_to([P, HPG, HD])
                    for c in range(NT):
                        ins = tt(yx[:, c, :].rearrange("p (h e) -> p h e", h=HPG),
                                 xtok[:, c, :].rearrange("p (h e) -> p h e", h=HPG), skip, ALU.mult)
                    ins.then_inc(yx_ready, 1)
                if one:
                    pool.wait_ge(diff_done, g * 2 + 1)
                    for c in range(NT):
                        for part, a_dt in ((uaH, adtH), (uaL, adtL)):
                            a_c = a_dt[:, bass.ds(g * HPG + c * HEADS, HPG)].bitcast(F32).unsqueeze(2)\
                                .broadcast_to([P, HPG, P])
                            ins = tt(part[:, c, :, :], upper[:, :].unsqueeze(1).broadcast_to([P, HPG, P]), a_c,
                                     ALU.mult)
                        ins.then_inc(ua_ready, 1)
                if not one:
                    ln_factors(0)
                if two:
                    pool.wait_ge(ssg_ready, g)
                    rsqrt(rG, ssG, inv_g, rg_ready)

            window(0, True, False)
            with pool.Fori(1, GROUPS) as g:
                order.enter(g, 3, 1)
                window(g, True, True)
            order.leave(GROUPS - 1)
            window(GROUPS, False, True)
            with pool.Fori(1, NBLK) as i:
                order.enter(i, 1, 1)
                ln_factors(i)
            order.leave(NBLK - 1)
            pool.wait_ge(sa_ready, 1)
            rsqrt(rA, sA, inv_d, ra_ready)
            with pool.Fori(0, NBLK) as n:
                pool.wait_ge(dve_evac, n * 2 + (V_O + 2) + 1)
                pool.tensor_copy(h3[:, :, bass.ds(n * NB, NB)], hb).then_inc(hcopy_done, 1)
            pool.memset(xf[:, :, 0:2], 0.0).then_inc(fpads_ready, 1)
            pool.wait_ge(sh_ready, 1)
            rsqrt(rH, sH, inv_d, rh_ready)
            pool.wait_ge(rh_ready, 1)
            for t in range(NT):
                pool.tensor_scalar(dg[:, t, :], ident[:, :], rH[:, t:t + 1], None, ALU.mult).then_inc(dg_ready, 1)
            with pool.Fori(0, NBLK // 2) as i:
                pool.wait_ge(dve_evac, i * 2 + (V_D + 1) + 1)
                pool.tensor_copy(h3[:, :, bass.ds(i * 2 * NB, NB)], hb).then_inc(hcopy_done, 1)
            pool.wait_ge(sp_ready, 1)
            rsqrt(rP, sP, inv_d, rp_ready)
            pool.wait_ge(sf_ready, 1)
            tt(rF, sF, half[:, 0:NT], ALU.pow).then_inc(rf_ready, 1)

        @block.scalar
        def _(act):
            for first in by_scalar:
                act.sem_inc(first, 1)
            fn = act.activation
            order = act_order

            def split(r, j):
                act.wait_ge(raw_in[j], r * 16 + 16)
                act.wait_ge(chunk_used, r * SLOTS + (j + 1 - SLOTS))
                fn(wH[:, j, :, :], raw[:, j, :, :], ACT.Copy).then_inc(wh_ready, 1)

            def splits(lo, hi):
                while lo < hi:
                    if lo % SLOTS == 0 and hi - lo >= 2 * SLOTS:
                        with act.Fori(lo // SLOTS, hi // SLOTS) as r:
                            for j in range(SLOTS):
                                split(r, j)
                        lo = hi // SLOTS * SLOTS
                    else:
                        split(lo // SLOTS, lo % SLOTS)
                        lo += 1

            def evac_high(dst, banks, k0, col):
                for m in range(BT):
                    ins = fn(dst[:, bass.ds(k0 + m, 1), :].rearrange("p a c -> p (a c)"),
                             ps[banks + m // 2][:, (m % 2) * SEQ:(m % 2 + 1) * SEQ], ACT.Copy,
                             scale=prm[:, bass.ds(k0 + (col + m), 1)])
                return ins

            act.wait_ge(const_ready, 5)
            fn(dg[:, 0, 0:1], ones[:, 0:1], ACT.Copy).then_inc(warm_ready, 1)
            act.wait_ge(gain_in, 16)
            for k in range(KD):
                if k in XT_CUTS:
                    act.wait_ge(xT_in[XT_CUTS.index(k)], 16)
                fn(aH[:, k, :], xTs[:, k, :], ACT.Copy, scale=prm[:, C_MIX + k:C_MIX + k + 1]).then_inc(ah_ready, 1)
                if k % 2 == 1:
                    j = k // 2 % SLOTS
                    if k < 2 * SLOTS:
                        act.wait_ge(raw_in[j], 16)
                        fn(wH[:, j, :, :], raw[:, j, :, :], ACT.Copy).then_inc(wh_ready, 1)
                    else:
                        split(1, j)
            split(2, 0)
            split(2, 1)
            act.wait_ge(ssmm_done, 1)
            fn(ss0, ps[7][:, 0:NT], ACT.Copy).then_inc(ss0_ready, 1)
            split(2, 2)
            split(2, 3)
            act.wait_ge(wdt_in, 16)
            fn(wdtH[:, :, 0:HEADS], wdtr[:, :, :], ACT.Copy).then_inc(wdth_ready, 1)
            act.wait_ge(prm_in, 16)

            act.wait_ge(r0_ready, 1)
            for b in range(NBLK):
                q0 = AHEAD + b * CB
                act.wait_ge(chunk_used, (b + 1) * CB)
                for t in range(NT):
                    ins = fn(z4[:, 2 * b:2 * b + 2, t, :], tok_bank(b, t)[:, :].rearrange("p (g c) -> p g c", g=2),
                             ACT.Silu, scale=r0[:, t:t + 1])
                ins.then_inc(act_evac, 1)
                if b < NBLK - 1:
                    splits(q0, q0 + CB)
                    continue
                act.wait_ge(dtmm_done, 1)
                fn(dtT[0:HEADS, :], ps[4][0:HEADS, 0:SEQ], ACT.Copy).then_inc(dtt_ready, 1)
                act.wait_ge(rbmm_done, 1)
                fn(rb[:, :], ps[6][:, 0:SEQ], ACT.Copy).then_inc(rb_ready, 1)
                splits(q0, q0 + 3)
                act.wait_ge(dtu_ready, 1)
                order.mark(fn(dte, dtu, ACT.Abs))
                act.wait_ge(rows_in, 16)
                order.wait(act)
                fn(dte, dte, ACT.Exp, scale=-1.0).then_inc(dte_ready, 1)
                fn(rows[:, 1, :], rows[:, 1, :], ACT.Exp).then_inc(dte_ready, 1)
                splits(q0 + 3, q0 + CB - 1)
                act.wait_ge(csmm_done, 1)
                fn(ea, ps[7][:, 0:NT * HEADS], ACT.Exp)
                fn(ed[:, :], ps[7][:, P:P + HEADS], ACT.Exp).then_inc(ea_ready, 1)
                splits(q0 + CB - 1, q0 + CB)

            def xtok_evac(g):
                act.wait_ge(xtr_done, g)
                act.wait_ge(yx_ready, g)
                fn(xtok[:, :, :].rearrange("p t c -> p (t c)"), ps[4][:, :], ACT.Copy).then_inc(tok_ready, 1)

            def state_evac(g):
                act.wait_ge(st_done, g)
                fn(stT[:, :], ps[4][:, 0:GC], ACT.Copy).then_inc(st_ready, 1)

            def gated_norm(g):
                act.wait_ge(y_ready, g + 1)
                for t in range(NT):
                    ins = fn(xs[:, t, 3:3 + GC], y[:, t, :], ACT.Square, accum_out=ssG[:, t:t + 1])
                ins.then_inc(ssg_ready, 1)
                act.wait_ge(rg_ready, g)
                for t in range(NT):
                    ins = fn(y[:, t, :], y[:, t, :], ACT.Copy, scale=rG[:, t:t + 1])
                ins.then_inc(yn_ready, 1)

            def y_evac(g):
                act.wait_ge(ytr_done, g)
                for m in range(2):
                    ins = fn(yBH[:, bass.ds(g * 2 + (m - 2), 1), :].rearrange("p a c -> p (a c)"),
                             ps[5][:, m * SEQ:(m + 1) * SEQ], ACT.Copy,
                             scale=prm[:, bass.ds(g * 2 + (C_SSM + m - 2), 1)])
                ins.then_inc(yh_ready, 1)

            def window(g, s, two):
                if two:
                    xtok_evac(g)
                act.wait_ge(dve_evac, g + (V_G + 1) + 1)
                if two:
                    act.wait_ge(ct_ready, g)
                    act.wait_ge(scores_done, g)
                for m in range(BT):
                    w = C_CONV + 5 * m
                    ins = fn(cv[:, m, :], xs[:, m, 3:3 + SEQ], ACT.Identity,
                             scale=prm[:, bass.ds(g * (5 * BT) + (w + 3), 1)],
                             bias=prm[:, bass.ds(g * (5 * BT) + (w + 4), 1)])
                ins.then_inc(cv0_ready, 1)
                s(0)
                s(1)
                if two:
                    state_evac(g)
                s(2)
                s(3)
                act.wait_ge(conv_ready, g + 1)
                fn(cv[:, :, :], cv[:, :, :], ACT.Silu).then_inc(silu_ready, 1)
                s(4)
                act.wait_ge(silu_ready, g + 1)
                act.wait_ge(y_done, g + 1)
                fn(ct[:, :], cv[:, 3, P:2 * P], ACT.Copy).then_inc(ct_ready, 1)
                if two:
                    gated_norm(g)
                s(5)
                for c in range(NT):
                    act.wait_ge(diff_done, g * 2 + (c + 1) + 1)
                    fn(E[:, c, :, :].rearrange("p h l -> p (h l)"), ps[6 + c][:, :], ACT.Exp).then_inc(exp_ready, 1)
                if two:
                    y_evac(g)
                s(6)
                s(7)

            window(0, lambda c: split(3 + 2 * G0 + c // 4, c % 4), False)
            with act.Fori(0, (GROUPS - 2) // 2) as i:
                for b in range(2):
                    window(i * 2 + (1 + b), lambda c: split(i * 4 + (5 + 2 * G0 + 2 * b + c // 4), c % 4), True)
            window(GROUPS - 1, lambda c: split(1 + 2 * V0 + c // 4, c % 4), True)

            def v_window(i, s, ssd):
                act.wait_ge(chunk_used, i * (2 * CB) + (V0 + 1) * CB)
                act.wait_ge(sg_done, i + 1)
                act.dma_start(wsT, wsT_d[i]).then_inc(ws_in, 16)
                act.dma_start(lnr, ln_d[i].partition_broadcast(P)).then_inc(ws_in, 16)
                if ssd:
                    xtok_evac(GROUPS)
                for t in range(NT):
                    ins = fn(v[:, t, :], tok_bank(0, t)[:, :], ACT.Gelu_apprx_tanh, scale=r0[:, t:t + 1])
                ins.then_inc(act_evac, 1)
                s(0, 2)
                if ssd:
                    state_evac(GROUPS)
                s(2, 5)
                if ssd:
                    gated_norm(GROUPS)
                s(5, 7)
                if ssd:
                    y_evac(GROUPS)
                s(7, CB)

            def load_residual(n):
                act.dma_start(h3[:, :, n * NB:(n + 1) * NB],
                              x.rearrange("(t p) d -> p t d", p=P)[:, :, n * NB:(n + 1) * NB])\
                    .then_inc(x2_in[n // 2], 16)

            def u_window(i, s, last):
                act.wait_ge(chunk_used, i * (2 * CB) + (V0 + 2) * CB)
                for t in range(NT):
                    ins = fn(u[:, t, :], tok_bank(1, t)[:, :], ACT.Gelu_apprx_tanh, scale=r0[:, t:t + 1])
                ins.then_inc(act_evac, 1)
                s(CB, CB + 3)
                act.wait_ge(ya_ready, i + 1)
                for t in range(NT):
                    ins = fn(v[:, t, :], u[:, t, :], ACT.Square, accum_out=ssA[:, t, bass.ds(i, 1)])
                ins.then_inc(ssa_ready, 1)
                if last:
                    act.wait_ge(ssa_ready, NBLK)
                    load_residual(0)
                    load_residual(1)
                s(CB + 3, CB + 5)
                act.wait_ge(yatr_done, i + 1)
                evac_high(yAH, 6, i * BT, C_A).then_inc(yah_ready, 1)
                s(CB + 5, 2 * CB)

            def vu_splits(i):
                def s(lo, hi):
                    for c in range(lo, hi):
                        split(i * 4 + (3 + 2 * V0 + c // 4), c % 4)
                return s

            v_window(0, vu_splits(0), True)
            u_window(0, vu_splits(0), False)
            with act.Fori(1, NBLK - 1) as i:
                v_window(i, vu_splits(i), False)
                u_window(i, vu_splits(i), False)
            v_window(NBLK - 1, vu_splits(NBLK - 1), False)
            u_window(NBLK - 1, vu_splits(NBLK - 1), True)
            load_residual(2)
            load_residual(3)

            with act.Fori(0, NBLK) as n:
                def s(lo, hi):
                    for c in range(lo, hi):
                        split(n * 4 + (3 + 2 * O0 + c // 4), c % 4)

                s(0, CB + 1)
                act.wait_ge(dve_evac, n * 2 + (V_O + 2) + 1)
                for t in range(NT):
                    ins = fn(junk[:, t, :], hb[:, t, :], ACT.Square, accum_out=ssH[:, t, bass.ds(n, 1)])
                ins.then_inc(ssh_ready, 1)
                s(CB + 1, CB + 3)
                act.wait_ge(htr_done, n + 1)
                evac_high(aH, 4, n * BT, C_FFN).then_inc(fh_ready, 1)
                s(CB + 3, 2 * CB)
            act.wait_ge(rbmm_done, 2)
            fn(rb[:, :], ps[6][:, 0:SEQ], ACT.Copy).then_inc(rb_ready, 1)

            act.wait_ge(hcopy_done, NBLK + 1)
            with act.Fori(0, FB) as i:
                for b, cf in enumerate((cfG, cfU)):
                    def s(lo, hi):
                        for c in range(lo, hi):
                            split(i * 4 + (3 + 2 * F0 + 2 * b + c // 4), c % 4)

                    s(0, 1)
                    act.wait_ge(dve_evac, i * 2 + (V_F + 1 + b) + 1)
                    act.wait_ge(gul_ready, i + 1)
                    for m in range(BT):
                        w = C_CONVF + 4 * (m + b * KF)
                        ins = fn(cf[:, m, :], xf[:, m, 2:2 + SEQ], ACT.Identity,
                                 scale=prm[:, bass.ds(i * (4 * BT) + (w + 2), 1)],
                                 bias=prm[:, bass.ds(i * (4 * BT) + (w + 3), 1)])
                    ins.then_inc(fc0_ready, 1)
                    s(1, 4)
                    if b == 0:
                        act.wait_ge(fconv_ready, i * 2 + 1)
                        fn(cfG[:, :, :], cfG[:, :, :], ACT.Silu).then_inc(fsilu_ready, 1)
                        s(4, 8)
                    else:
                        s(4, 5)
                        act.wait_ge(gu_ready, i + 1)
                        fn(guH[:, bass.ds(i * BT, BT), :], cfU[:, :, :], ACT.Copy).then_inc(guh_ready, 1)
                        s(5, 8)

            act.wait_ge(fconv_ready, 2 * FB)
            act.dma_start(praw, pT_d).then_inc(p_in, 16)
            q = CHUNK_D + AHEAD
            splits(q, q + 4)
            act.wait_ge(p_in, 16)
            fn(pH[:, :, :], praw, ACT.Copy).then_inc(ph_ready, 1)
            splits(q + 4, CHUNK_D + CF + SLOTS)

            for n in range(NBLK):
                q = CHUNK_D + (n + 1) * CF + SLOTS
                splits(q, q + 1)
                act.wait_ge(dve_evac, V_D + 1 + n + 1)
                for t in range(NT):
                    src = h3[:, t, n * NB:(n + 1) * NB] if n % 2 else hb[:, t, :]
                    ins = fn(junk[:, t, :], src, ACT.Square, accum_out=ssP[:, t, n:n + 1])
                ins.then_inc(ssp_ready, 1)
                if n % 2 == 0:
                    splits(q + 1, q + 6)
                    act.wait_ge(htr_done, NBLK + 1 + n // 2)
                    evac_high(aH, 4, n * BT, C_PLE).then_inc(fh_ready, 1)
                    splits(q + 6, q + CF)
                elif n < NBLK - 1:
                    splits(q + 1, q + CF)
            q += 1

            for n in range(NBLK):
                act.wait_ge(chunk_used, CHUNK_P + n + 1)
                for t in range(NT):
                    ins = fn(pw[:, t, n * NB:(n + 1) * NB], tok_bank(n, t)[:, :], ACT.Copy)
                ins.then_inc(act_evac, 1)
                if n == 0:
                    act.dma_start(gf[:, :], gf_d.partition_broadcast(P)).then_inc(gf_in, 16)
                if n == 1:
                    act.wait_ge(htr_done, NBLK + 3)
                    evac_high(aH, 4, 1 * BT, C_PLE).then_inc(fh_ready, 1)
                if n < NBLK - 1:
                    splits(q, q + 1)
                    q += 1
            act.wait_ge(htr_done, NBLK + 4)
            evac_high(aH, 4, 3 * BT, C_PLE).then_inc(fh_ready, 1)
            splits(q, q + CB)
            q += CB

            act.wait_ge(rp_ready, 1)
            for n in range(NBLK - 1):
                act.wait_ge(chunk_used, CHUNK_E + (n + 1) * CB)
                act.wait_ge(hf_ready, n)
                for t in range(NT):
                    ins = fn(gate[:, t, :], tok_bank(n, t)[:, :], ACT.Sigmoid, scale=rP[:, t:t + 1])
                ins.then_inc(act_evac, 1)
                act.wait_ge(hf_ready, n + 1)
                for t in range(NT):
                    ins = fn(junk[:, t, :], h3[:, t, n * NB:(n + 1) * NB], ACT.Square, accum_out=ssF[:, t, n:n + 1])
                ins.then_inc(ssf_ready, 1)
                hi = min(q + CB, CHUNKS)
                splits(q, hi)
                q = hi
            act.wait_ge(hf_ready, NBLK - 1)
            for t in range(NT):
                if t == 0:
                    act.wait_ge(e0_done, 1)
                else:
                    act.wait_ge(chunk_used, CHUNKS)
                fn(gate[:, t, :], tok_bank(NBLK - 1, t)[:, :], ACT.Sigmoid, scale=rP[:, t:t + 1]).then_inc(act_evac, 1)
            for t in range(NT):
                act.wait_ge(hf_ready, NBLK + t)
                fn(junk[:, t, :], h3[:, t, D - NB:D], ACT.Square, accum_out=ssF[:, t, NBLK - 1:NBLK])\
                    .then_inc(ssf_ready, 1)
            act.wait_ge(hg_ready, 1)
            act.wait_ge(rf_ready, 1)
            for half in range(2):
                blk = slice(half * D // 2, (half + 1) * D // 2)
                fn(pw[:, 1, blk], pw[:, 1, blk], ACT.Copy, scale=rF[:, 1:2]).then_inc(out1_ready, 1)

        @block.vector
        def _(dve):
            for first in by_vector:
                dve.sem_inc(first, 1)
            tt, stt, ts = dve.tensor_tensor, dve.scalar_tensor_tensor, dve.tensor_scalar
            order = dve_order

            def split(r, j):
                dve.wait_ge(wh_ready, r * SLOTS + (j + 1))
                tt(wL[:, j, :, :], raw[:, j, :, :], wH[:, j, :, :].bitcast(F32), ALU.subtract).then_inc(wl_ready, 1)

            def splits(lo, hi):
                while lo < hi:
                    if lo % SLOTS == 0 and hi - lo >= 2 * SLOTS:
                        with dve.Fori(lo // SLOTS, hi // SLOTS) as r:
                            for j in range(SLOTS):
                                split(r, j)
                        lo = hi // SLOTS * SLOTS
                    else:
                        split(lo // SLOTS, lo % SLOTS)
                        lo += 1

            def evac_low(dst, high, banks, k0, col):
                for m in range(BT):
                    ins = stt(dst[:, bass.ds(k0 + m, 1), :].rearrange("p a c -> p (a c)"),
                              ps[banks + m // 2][:, (m % 2) * SEQ:(m % 2 + 1) * SEQ],
                              prm[:, bass.ds(k0 + (col + m), 1)],
                              high[:, bass.ds(k0 + m, 1), :].rearrange("p a c -> p (a c)").bitcast(F32),
                              ALU.mult, ALU.subtract)
                return ins

            dve.wait_ge(gain_in, 16)
            for k in range(KD):
                if k in XT_CUTS:
                    dve.wait_ge(xT_in[XT_CUTS.index(k)], 16)
                dve.wait_ge(ah_ready, k + 1)
                stt(aL[:, k, :], xTs[:, k, :], prm[:, C_MIX + k:C_MIX + k + 1], aH[:, k, :].bitcast(F32),
                    ALU.mult, ALU.subtract).then_inc(al_ready, 1)
                if k % 2 == 1:
                    split(k // 2 // SLOTS, k // 2 % SLOTS)
            splits(2 * SLOTS, AHEAD)
            dve.wait_ge(prm_in, 16)
            dve.wait_ge(wdth_ready, 1)
            tt(wdtL[:, :, 0:HEADS], wdtr[:, :, :], wdtH[:, :, 0:HEADS].bitcast(F32),
               ALU.subtract).then_inc(wdtl_ready, 1)
            splits(AHEAD, AHEAD + (NBLK - 1) * CB)

            q = AHEAD + (NBLK - 1) * CB
            splits(q, q + 2)
            dve.wait_ge(dttr_done, 1)
            dve.wait_ge(r0_ready, 1)
            dve.wait_ge(rows_in, 16)
            for t in range(NT):
                ins = stt(dtu[:, t * HEADS:(t + 1) * HEADS], ps[5][:, t * HEADS:(t + 1) * HEADS], r0[:, t:t + 1], rows[:, 0, :],
                          ALU.mult, ALU.add)
            ins.then_inc(dtu_ready, 1)
            splits(q + 2, q + 4)
            dve.wait_ge(dte_ready, 2)
            order.mark(ts(dtq, dte, 2.0, None, ALU.add))
            order.wait(dve)
            order.mark(dve.reciprocal(dtq, dtq))
            order.wait(dve)
            order.mark(tt(dte, dte, dtq, ALU.mult))
            order.wait(dve)
            order.mark(tt(dtq, dte, dte, ALU.mult))
            order.wait(dve)
            terms = 8
            order.mark(ts(acc, dtq, 1.0 / (2 * terms + 1), None, ALU.mult))
            for n in range(terms - 1, 0, -1):
                order.wait(dve)
                order.mark(stt(acc, acc, 1.0 / (2 * n + 1), dtq, ALU.add, ALU.mult))
            order.wait(dve)
            order.mark(stt(acc, acc, 1.0, dte, ALU.add, ALU.mult))
            order.mark(ts(dtu, dtu, 0.0, None, ALU.max))
            order.wait(dve)
            order.mark(stt(dt, acc, 2.0, dtu, ALU.mult, ALU.add))
            order.wait(dve)
            for t in range(NT):
                ins = stt(adt[:, t * HEADS:(t + 1) * HEADS], dt[:, t * HEADS:(t + 1) * HEADS], -1.0, rows[:, 1, :],
                          ALU.mult, ALU.mult)
            ins.then_inc(adt_ready, 1)
            dve.wait_ge(adt_ready, 1)
            order.mark(dve.tensor_copy(adtH[:, :], adt))
            order.wait(dve)
            tt(adtL[:, :], adt, adtH[:, :].bitcast(F32), ALU.subtract).then_inc(adt_ready, 1)
            splits(q + 4, q + CB)

            dve.wait_ge(rb_ready, 1)
            dve.wait_ge(pads_ready, 1)
            dve.wait_ge(ea_ready, 1)
            rb2 = rb[:, :].unsqueeze(1).broadcast_to([P, 2, SEQ])

            def products_evac(g):
                dve.wait_ge(scores_done, g)
                dve.tensor_copy(btok[:, :], ps[5][:, 0:P]).then_inc(btok_ready, 1)
                order.mark(tt(sc[:, :, :], ps[5][:, P:3 * P].rearrange("p (c l) -> p c l", c=NT),
                              upper[:, :].unsqueeze(1).broadcast_to([P, NT, P]), ALU.mult))
                dve.wait_ge(exp_ready, g * 2)
                order.wait(dve)
                for c in range(NT):
                    ins = tt(E[:, c, :, :], E[:, c, :, :], sc[:, c, :].unsqueeze(1).broadcast_to([P, HPG, P]),
                             ALU.mult)
                ins.then_inc(m_ready, 1)

            def output(g):
                dve.wait_ge(y_done, g + 1)
                dve.wait_ge(yx_ready, g + 1)
                order.mark(tt(y[:, :, :].rearrange("p t c -> p (t c)"), ps[6][:, :],
                              yx[:, :, :].rearrange("p t c -> p (t c)"), ALU.add))
                order.mark(tt(yo[:, :].rearrange("p (h e) -> p h e", h=HPG),
                              ps[7][:, 0:GC].rearrange("p (h e) -> p h e", h=HPG),
                              ea[:, bass.ds(g * HPG + (HEADS - HPG), HPG)].unsqueeze(2).broadcast_to([P, HPG, HD]),
                              ALU.mult))
                order.wait(dve)
                order.mark(tt(y[:, 1, :], y[:, 1, :], yo[:, :], ALU.add))
                order.wait(dve)
                tt(y[:, :, :], y[:, :, :], z4[:, bass.ds(g - 1, 1), :, :].rearrange("p g t c -> p (g t) c"),
                   ALU.mult).then_inc(y_ready, 1)

            def y_evac(g):
                dve.wait_ge(yh_ready, g)
                for m in range(2):
                    k = bass.ds(g * 2 + (m - 2), 1)
                    ins = stt(yBL[:, k, :].rearrange("p a c -> p (a c)"), ps[5][:, m * SEQ:(m + 1) * SEQ],
                              prm[:, bass.ds(g * 2 + (C_SSM + m - 2), 1)],
                              yBH[:, k, :].rearrange("p a c -> p (a c)").bitcast(F32), ALU.mult, ALU.subtract)
                ins.then_inc(yl_ready, 1)

            def window(g, b, s, two):
                dve.wait_ge(chunk_used, g * CB + (G0 + 1) * CB)
                for n in range(2):
                    ins = tt(xs[:, 2 * n:2 * n + 2, 3:3 + SEQ],
                             ps[2 * b + n][:, :].rearrange("p (m c) -> p m c", m=2), rb2, ALU.mult)
                ins.then_inc(dve_evac, 1)
                if two:
                    products_evac(g)
                s(0)
                dve.wait_ge(cv0_ready, g + 1)
                for tap in (2, 1, 0):
                    for m in range(BT):
                        ins = stt(cv[:, m, :], xs[:, m, tap:tap + SEQ],
                                  prm[:, bass.ds(g * (5 * BT) + (C_CONV + 5 * m + tap), 1)], cv[:, m, :],
                                  ALU.mult, ALU.add)
                    if tap:
                        order.mark(ins)
                        order.wait(dve)
                    else:
                        ins.then_inc(conv_ready, 1)
                    if tap == 1 and not two:
                        s(1)
                if two:
                    s(1)
                s(2)
                if two:
                    output(g)
                for c in range(3, 6):
                    s(c)
                if two:
                    y_evac(g)
                s(6)
                s(7)

            window(0, 0, lambda c: split(3 + 2 * G0 + c // 4, c % 4), False)
            with dve.Fori(0, (GROUPS - 2) // 2) as i:
                order.enter(i, 12)
                for b in range(2):
                    window(i * 2 + (1 + b), 1 - b, lambda c: split(i * 4 + (5 + 2 * G0 + 2 * b + c // 4), c % 4), True)
            order.leave((GROUPS - 2) // 2)
            window(GROUPS - 1, 1, lambda c: split(1 + 2 * V0 + c // 4, c % 4), True)

            def v_window(i, s, ssd):
                if ssd:
                    products_evac(GROUPS)
                s(0, 1)
                dve.wait_ge(act_evac, i * 2 + (A_VU + 1))
                for t in range(NT):
                    for gg in range(BT):
                        ins = dve.bn_stats(bst[:, t * BT + gg, :], v[:, t, gg * P:(gg + 1) * P])
                order.mark(ins)
                order.wait(dve)
                s(1, 2)
                for n in range(NT * BT):
                    ins = dve.bn_aggr(mv[:, n, :], bst[:, n, :])
                ins.then_inc(mv_ready, 1)
                s(2, 3)
                dve.wait_ge(rs_ready, i * 2 + 2)
                for t in range(NT):
                    for gg in range(BT):
                        n = t * BT + gg
                        ins = ts(v[:, t, gg * P:(gg + 1) * P], v[:, t, gg * P:(gg + 1) * P],
                                 rs[:, n:n + 1], nm[:, n:n + 1], ALU.mult, ALU.subtract)
                order.mark(ins)
                s(3, 4)
                if ssd:
                    output(GROUPS)
                dve.wait_ge(ws_in, i * 32 + 32)
                order.wait(dve)
                order.mark(tt(v, v, lnr[:, 0, :].unsqueeze(1).broadcast_to([P, NT, NB]), ALU.mult))
                order.wait(dve)
                tt(v, v, lnr[:, 1, :].unsqueeze(1).broadcast_to([P, NT, NB]), ALU.add).then_inc(vn_ready, 1)
                s(4, 7)
                if ssd:
                    y_evac(GROUPS)
                s(7, CB)

            def u_window(i, s):
                s(CB, CB + 1)
                dve.wait_ge(act_evac, i * 2 + (A_VU + 2))
                dve.wait_ge(sg_done, i + 2)
                for t in range(NT):
                    for gg in range(BT):
                        ins = stt(u[:, t, gg * P:(gg + 1) * P], ps[4 + t][:, gg * P:(gg + 1) * P],
                                  prm[:, bass.ds(i * BT + (C_BS + gg), 1)], u[:, t, gg * P:(gg + 1) * P],
                                  ALU.add, ALU.mult)
                ins.then_inc(ya_ready, 1)
                s(CB + 1, CB + 6)
                dve.wait_ge(yah_ready, i + 1)
                evac_low(yAL, yAH, 6, i * BT, C_A).then_inc(yal_ready, 1)
                s(CB + 6, 2 * CB)

            def vu_splits(i):
                def s(lo, hi):
                    for c in range(lo, hi):
                        split(i * 4 + (3 + 2 * V0 + c // 4), c % 4)
                return s

            v_window(0, vu_splits(0), True)
            u_window(0, vu_splits(0))
            with dve.Fori(1, NBLK) as i:
                order.enter(i, 3, 1)
                v_window(i, vu_splits(i), False)
                u_window(i, vu_splits(i))
            order.leave(NBLK - 1)
            dve.wait_ge(ssa_ready, NBLK)
            dve.reduce_sum(sA, ssA, AX.X).then_inc(sa_ready, 1)

            dve.wait_ge(ra_ready, 1)
            def o_window(n):
                def s(lo, hi):
                    for c in range(lo, hi):
                        split(n * 4 + (3 + 2 * O0 + c // 4), c % 4)

                dve.wait_ge(chunk_used, n * (2 * CB) + (O0 + 1) * CB)
                dve.wait_ge(hcopy_done, n + 1)
                dve.wait_ge(ssh_ready, n + 1)
                for t in range(NT):
                    ins = tt(hb[:, t, :], tok_bank(0, t)[:, :], h3[:, t, bass.ds(n * NB, NB)], ALU.add)
                ins.then_inc(dve_evac, 1)
                s(0, CB)
                dve.wait_ge(chunk_used, n * (2 * CB) + (O0 + 2) * CB)
                for t in range(NT):
                    ins = stt(hb[:, t, :], tok_bank(1, t)[:, :], rA[:, t:t + 1], hb[:, t, :], ALU.mult, ALU.add)
                ins.then_inc(dve_evac, 1)
                s(CB, CB + 4)
                dve.wait_ge(fh_ready, n + 1)
                evac_low(aL, aH, 4, n * BT, C_FFN).then_inc(fl_ready, 1)
                s(CB + 4, 2 * CB)
            dve.wait_ge(x2_in[0], 32)
            o_window(0)
            dve.wait_ge(x2_in[1], 32)
            with dve.Fori(1, NBLK) as n:
                o_window(n)
            dve.wait_ge(ssh_ready, NBLK + 1)
            dve.reduce_sum(sH, ssH, AX.X).then_inc(sh_ready, 1)

            dve.wait_ge(rb_ready, 2)
            dve.wait_ge(fpads_ready, 1)
            with dve.Fori(0, FB) as i:
                order.enter(i, 2)
                for b, cf in enumerate((cfG, cfU)):
                    def s(lo, hi):
                        for c in range(lo, hi):
                            split(i * 4 + (3 + 2 * F0 + 2 * b + c // 4), c % 4)

                    dve.wait_ge(chunk_used, i * (2 * CB) + (F0 + 1 + b) * CB)
                    for n in range(2):
                        ins = tt(xf[:, 2 * n:2 * n + 2, 2:2 + SEQ],
                                 ps[2 * b + n][:, :].rearrange("p (m c) -> p m c", m=2), rb2, ALU.mult)
                    ins.then_inc(dve_evac, 1)
                    s(0, 2)
                    dve.wait_ge(fc0_ready, i * 2 + (b + 1))
                    for tap in (1, 0):
                        for m in range(BT):
                            ins = stt(cf[:, m, :], xf[:, m, tap:tap + SEQ],
                                      prm[:, bass.ds(i * (4 * BT) + (C_CONVF + 4 * (m + b * KF) + tap), 1)],
                                      cf[:, m, :], ALU.mult, ALU.add)
                        if tap:
                            order.mark(ins)
                            s(2, 3)
                            order.wait(dve)
                        else:
                            ins.then_inc(fconv_ready, 1)
                    s(3, 4)
                    if b == 0:
                        s(4, 8)
                        continue
                    dve.wait_ge(fsilu_ready, i + 1)
                    dve.wait_ge(fconv_ready, i * 2 + 2)
                    tt(cfU[:, :, :], cfU[:, :, :], cfG[:, :, :], ALU.mult).then_inc(gu_ready, 1)
                    s(4, 6)
                    dve.wait_ge(guh_ready, i + 1)
                    tt(guL[:, bass.ds(i * BT, BT), :], cfU[:, :, :], guH[:, bass.ds(i * BT, BT), :].bitcast(F32),
                       ALU.subtract).then_inc(gul_ready, 1)
                    s(6, 8)
                order.leave(FB)

            q = CHUNK_D + AHEAD
            splits(q, q + 4)
            dve.wait_ge(ph_ready, 1)
            tt(pL[:, :, :], praw, pH[:, :, :].bitcast(F32), ALU.subtract).then_inc(pl_ready, 1)
            splits(q + 4, CHUNK_D + CF + SLOTS)

            for n in range(NBLK):
                q = CHUNK_D + (n + 1) * CF + SLOTS
                dve.wait_ge(chunk_used, CHUNK_D + (n + 1) * CF)
                dve.wait_ge(hcopy_done, NBLK + (n + 1) // 2 + 1)
                for t in range(NT):
                    src = h3[:, t, n * NB:(n + 1) * NB]
                    ins = tt(src if n % 2 else hb[:, t, :], tok_bank(n, t)[:, :], src, ALU.add)
                ins.then_inc(dve_evac, 1)
                splits(q, q + 1)
                if n % 2 == 0:
                    splits(q + 1, q + 7)
                    dve.wait_ge(fh_ready, NBLK + 1 + n // 2)
                    evac_low(aL, aH, 4, n * BT, C_PLE).then_inc(fl_ready, 1)
                    splits(q + 7, q + CF)
                elif n < NBLK - 1:
                    splits(q + 1, q + CF)
            q += 1
            dve.wait_ge(ssp_ready, NBLK)
            dve.reduce_sum(sP, ssP, AX.X).then_inc(sp_ready, 1)
            for n in range(1, NBLK):
                splits(q, q + 1)
                q += 1
                if n == 1:
                    dve.wait_ge(fh_ready, NBLK + 3)
                    evac_low(aL, aH, 4, 1 * BT, C_PLE).then_inc(fl_ready, 1)
            dve.wait_ge(fh_ready, NBLK + 4)
            evac_low(aL, aH, 4, 3 * BT, C_PLE).then_inc(fl_ready, 1)
            splits(q, q + CB)
            q += CB

            dve.wait_ge(gf_in, 16)
            for n in range(NBLK - 1):
                blk = slice(n * NB, (n + 1) * NB)
                dve.wait_ge(act_evac, A_E + n + 1)
                order.mark(tt(gate[:, :, :], gate[:, :, :], pw[:, :, blk], ALU.mult))
                order.wait(dve)
                tt(h3[:, :, blk], h3[:, :, blk], gate[:, :, :], ALU.add).then_inc(hf_ready, 1)
                hi = min(q + CB, CHUNKS)
                splits(q, hi)
                q = hi
                dve.wait_ge(hf_ready, n + 1)
                tt(pw[:, :, blk], h3[:, :, blk], gf[:, blk].unsqueeze(1).broadcast_to([P, NT, NB]), ALU.mult)
            blk = slice(D - NB, D)
            for t in range(NT):
                dve.wait_ge(act_evac, A_E + NBLK + t)
                order.mark(tt(gate[:, t, :], gate[:, t, :], pw[:, t, blk], ALU.mult))
                order.wait(dve)
                tt(h3[:, t, blk], h3[:, t, blk], gate[:, t, :], ALU.add).then_inc(hf_ready, 1)
            dve.wait_ge(hf_ready, NBLK + 1)
            tt(pw[:, :, blk], h3[:, :, blk], gf[:, blk].unsqueeze(1).broadcast_to([P, NT, NB]),
               ALU.mult).then_inc(hg_ready, 1)
            dve.wait_ge(ssf_ready, NBLK + 1)
            order.mark(dve.reduce_sum(sF, ssF, AX.X))
            order.wait(dve)
            ts(sF, sF, 1.0 / D, EPS, ALU.mult, ALU.add).then_inc(sf_ready, 1)
            dve.wait_ge(hg_ready, 1)
            dve.wait_ge(rf_ready, 1)
            for half in range(2):
                blk = slice(half * D // 2, (half + 1) * D // 2)
                ts(pw[:, 0, blk], pw[:, 0, blk], rF[:, 0:1], None, ALU.mult).then_inc(out0_ready, 1)

        @block.tensor
        def _(pe):
            for first in by_tensor:
                pe.sem_inc(first, 1)
            mm = pe.matmul

            def tok_chunk(chunk, slot, high, low, k0, blk, first, last, tile_done=None):
                pe.wait_ge(wl_ready, chunk + 1)
                for t in range(NT):
                    tok = slice(t * P, (t + 1) * P)
                    for kk in range(KC):
                        for n, (a, w) in enumerate(((high, wH), (high, wL), (low, wH))):
                            ins = mm(tok_bank(blk, t)[:, :], a[:, k0 + kk, tok], w[:, slot, kk, :],
                                     start=first and kk == 0 and n == 0, stop=last and kk == KC - 1 and n == 2)
                    if t == 0 and tile_done is not None:
                        ins.then_inc(tile_done, 1)
                ins.then_inc(chunk_used, 1)

            def ch_chunk(chunk, slot, k0, blk, first, last):
                pe.wait_ge(wl_ready, chunk + 1)
                for kk in range(KC):
                    for m in range(BT):
                        out_m = ps[2 * (blk % 2) + m // 2][:, (m % 2) * SEQ:(m % 2 + 1) * SEQ]
                        for n, (w, a) in enumerate(((wH, aH), (wH, aL), (wL, aH))):
                            ins = mm(out_m, w[:, slot, kk, m * P:(m + 1) * P], a[:, k0 + kk, :],
                                     start=first and kk == 0 and n == 0 and m % 2 == 0,
                                     stop=last and kk == KC - 1 and n == 2, skip_group_check=True)
                ins.then_inc(chunk_used, 1)

            def transposes(src, banks):
                for m in range(BT):
                    for t in range(NT):
                        ins = pe.transpose(ps[banks + m // 2][:, (m % 2) * SEQ + t * P:(m % 2) * SEQ + (t + 1) * P],
                                           src[:, t, m * P:(m + 1) * P], ident[:, :])
                return ins

            def spread(n):
                pe.wait_ge(dg_ready, n * NT)
                mm(ps[6][:, 0:SEQ], ones[:, :], dg[:, :, :].rearrange("p t c -> p (t c)"), start=True,
                   stop=True).then_inc(rbmm_done, 1)

            def ssd_decays(g):
                pe.wait_ge(y_ready, g + 1)
                for c in range(NT):
                    pe.wait_ge(ua_ready, g * 2 + (c + 1))
                    mm(ps[6 + c][:, :], lowerR[:, :], uaH[:, c, :, :].rearrange("p h l -> p (h l)"),
                       start=True, stop=False)
                    mm(ps[6 + c][:, :], lowerR[:, :], uaL[:, c, :, :].rearrange("p h l -> p (h l)"),
                       start=False, stop=True).then_inc(diff_done, 1)

            def ssd_scores(g):
                pe.wait_ge(silu_ready, g + 1)
                pe.wait_ge(st_ready, g + 1)
                for t in range(NT):
                    pe.transpose(ps[4][:, t * GC:t * GC + P], cv[:, 0, t * P:(t + 1) * P], ident[:, :])
                    ins = pe.transpose(ps[4][:, t * GC + P:(t + 1) * GC], cv[:, 1, t * P:(t + 1) * P], ident[:, :])
                ins.then_inc(xtr_done, 1)
                pe.wait_ge(yl_ready, g + 1)
                pe.transpose(ps[5][:, 0:P], cv[:, 2, 0:P], ident[:, :])
                for c in range(NT):
                    chunk = slice(c * P, (c + 1) * P)
                    ins = mm(ps[5][:, (c + 1) * P:(c + 2) * P], cv[:, 2, chunk], cv[:, 3, chunk], start=True, stop=True)
                ins.then_inc(scores_done, 1)

            def ssd_states(g):
                pe.wait_ge(btok_ready, g + 1)
                pe.wait_ge(xd_ready, g + 1)
                mm(ps[4][:, 0:GC], btok[:, :], xdd[:, :], start=True, stop=True).then_inc(st_done, 1)

            def ssd_outputs(g):
                pe.wait_ge(ct_ready, g + 1)
                pe.wait_ge(m_ready, g + 1)
                pe.wait_ge(st_ready, g + 1 + 1)
                for c in range(NT):
                    for hh in range(HPG):
                        mm(ps[6][:, c * GC + hh * HD:c * GC + (hh + 1) * HD], E[:, c, hh, :],
                           xdt[:, c, hh * HD:(hh + 1) * HD], start=True, stop=True)
                mm(ps[7][:, 0:GC], ct[:, :], stT[:, :], start=True, stop=True).then_inc(y_done, 1)

            def ssd_transposes(g):
                pe.wait_ge(yn_ready, g + 1)
                for m in range(2):
                    for t in range(NT):
                        ins = pe.transpose(ps[5][:, m * SEQ + t * P:m * SEQ + (t + 1) * P], y[:, t, m * P:(m + 1) * P],
                                           ident[:, :])
                ins.then_inc(ytr_done, 1)

            pe.wait_ge(const_ready, 7)
            for _ in range(WARM):
                mm(ps[7][:, 0:P], ones[:, :], ident[:, :], start=True, stop=True)

            for b in range(NBLK):
                if b >= 2:
                    pe.wait_ge(act_evac, A_Z + b - 1)
                for c in range(CB):
                    if b == 0:
                        pe.wait_ge(al_ready, 2 * c + 2)
                    tok_chunk(b * CB + c, c % SLOTS, aH, aL, KC * c, b, c == 0, c == CB - 1)
                    if b == 0 and c == 5:
                        pe.wait_ge(sq_ready, 1)
                        for t in range(NT):
                            ins = mm(ps[7][:, t:t + 1], sqa[:, 0, t * P:(t + 1) * P], ones[:, 0:1], start=True,
                                     stop=True)
                        ins.then_inc(ssmm_done, 1)
            pe.wait_ge(wdtl_ready, 1)
            pe.wait_ge(wpad_ready, 2)
            for k in range(KD):
                for n, (w, a) in enumerate(((wdtH, aH), (wdtH, aL), (wdtL, aH))):
                    ins = mm(ps[4][:, 0:SEQ], w[:, k, :], a[:, k, :], start=k == 0 and n == 0,
                             stop=k == KD - 1 and n == 2)
            ins.then_inc(dtmm_done, 1)
            spread(1)
            pe.wait_ge(act_evac, A_Z + 3)
            for c in range(CB):
                ch_chunk(G0 * CB + c, c % SLOTS, KC * c, G0, c == 0, c == CB - 1)
                if c == 0:
                    pe.wait_ge(dtt_ready, 1)
                    for t in range(NT):
                        ins = pe.transpose(ps[5][:, t * HEADS:(t + 1) * HEADS], dtT[0:HEADS, t * P:(t + 1) * P],
                                           ident[0:HEADS, 0:HEADS])
                    ins.then_inc(dttr_done, 1)
                if c == 6:
                    pe.wait_ge(adt_ready, 1)
                    mm(ps[7][:, 0:NT * HEADS], upper[:, :], adt, start=True, stop=True)
                    mm(ps[7][:, P:P + HEADS], lower[:, :], adt[:, 0:HEADS], start=True, stop=True)\
                        .then_inc(csmm_done, 1)

            def with_ssd(g, one, two, block_chunk):
                for c in range(CB):
                    block_chunk(c)
                    if c == 1 and two:
                        ssd_states(g - 1)
                    if c == 3 and two:
                        ssd_outputs(g - 1)
                    if c == 5 and one:
                        ssd_decays(g)
                    if c == 6 and two:
                        ssd_transposes(g - 1)
                    if c == 7 and one:
                        ssd_scores(g)

            def g_block(g, blk, two):
                with_ssd(g, True, two, lambda c: ch_chunk(g * CB + ((G0 + 1) * CB + c), c % SLOTS, KC * c, blk,
                                                          c == 0, c == CB - 1))

            pe.wait_ge(act_evac, A_Z + 4)
            g_block(0, 1, False)
            with pe.Fori(0, (GROUPS - 2) // 2) as i:
                for b in range(2):
                    pe.wait_ge(dve_evac, i * 2 + (b + 2))
                    g_block(i * 2 + (1 + b), b, True)

            def vu_block(i, b, side):
                for c in range(CB):
                    tok_chunk(i * (2 * CB) + ((V0 + b) * CB + c), c % SLOTS, aH, aL, KC * c, b, c == 0, c == CB - 1)
                    side(c)

            def spatial(i):
                pe.wait_ge(vn_ready, i + 1)
                pe.wait_ge(ws_ready, i + 1)
                for t in range(NT):
                    for gg in range(BT):
                        ins = mm(ps[4 + t][:, gg * P:(gg + 1) * P], wsT[:, gg, :], v[:, t, gg * P:(gg + 1) * P],
                                 start=True, stop=True)
                ins.then_inc(sg_done, 1)

            def ya_transposes(i):
                pe.wait_ge(ya_ready, i + 1)
                pe.wait_ge(yal_ready, i + 1)
                transposes(u, 6).then_inc(yatr_done, 1)

            pe.wait_ge(dve_evac, V_G + GROUPS)
            with_ssd(GROUPS - 1, True, True,
                     lambda c: tok_chunk(V0 * CB + c, c % SLOTS, aH, aL, KC * c, 0, c == 0, c == CB - 1))
            pe.wait_ge(dve_evac, V_G + GROUPS + 1)
            with_ssd(GROUPS, False, True,
                     lambda c: tok_chunk((V0 + 1) * CB + c, c % SLOTS, aH, aL, KC * c, 1, c == 0, c == CB - 1))
            pe.wait_ge(yl_ready, GROUPS + 1)
            spatial(0)
            pe.wait_ge(act_evac, A_VU + 1)
            vu_block(1, 0, lambda c: ya_transposes(0) if c == 4 else None)
            with pe.Fori(1, NBLK - 1) as i:
                pe.wait_ge(act_evac, i * 2 + A_VU)
                vu_block(i, 1, lambda c: spatial(i) if c == 6 else None)
                pe.wait_ge(act_evac, i * 2 + (A_VU + 1))
                vu_block(i + 1, 0, lambda c: ya_transposes(i) if c == 4 else None)
            pe.wait_ge(act_evac, A_VU + 2 * NBLK - 2)
            vu_block(NBLK - 1, 1, lambda c: spatial(NBLK - 1) if c == 6 else None)

            def o_block(n, b, side):
                for c in range(CB):
                    tok_chunk(n * (2 * CB) + ((O0 + b) * CB + c), c % SLOTS, (yBH, yAH)[b], (yBL, yAL)[b], KC * c, b,
                              c == 0, c == CB - 1)
                    side(c)

            def h_transposes(n):
                pe.wait_ge(dve_evac, n * 2 + (V_O + 2) + 1)
                pe.wait_ge(fl_ready, n + 1)
                transposes(hb, 4).then_inc(htr_done, 1)

            pe.wait_ge(act_evac, A_VU + 2 * NBLK - 1)
            o_block(0, 0, lambda c: ya_transposes(NBLK - 1) if c == 4 else None)
            pe.wait_ge(act_evac, A_VU + 2 * NBLK)
            pe.wait_ge(yal_ready, NBLK + 1)
            o_block(0, 1, lambda c: None)
            with pe.Fori(1, NBLK) as n:
                pe.wait_ge(dve_evac, n * 2 + (V_O - 1) + 1)
                o_block(n, 0, lambda c: h_transposes(n - 1) if c == 2 else None)
                pe.wait_ge(dve_evac, n * 2 + V_O + 1)
                o_block(n, 1, lambda c: None)

            def f_block(i, b, side):
                for c in range(CB):
                    ch_chunk(i * (2 * CB) + ((F0 + b) * CB + c), c % SLOTS, KC * c, b, c == 0, c == CB - 1)
                    side(c)

            def first_side(c):
                if c == 2:
                    h_transposes(NBLK - 1)
                if c == 5:
                    pe.wait_ge(fl_ready, NBLK + 1)

            pe.wait_ge(dve_evac, V_O + 2 * NBLK - 1 + 1)
            pe.wait_ge(fl_ready, NBLK - 1 + 1)
            f_block(0, 0, first_side)
            pe.wait_ge(dve_evac, V_O + 2 * NBLK + 1)
            f_block(0, 1, lambda c: spread(2) if c == 1 else None)
            with pe.Fori(1, FB) as i:
                pe.wait_ge(dve_evac, i * 2 + (V_F - 1) + 1)
                f_block(i, 0, lambda c: None)
                pe.wait_ge(dve_evac, i * 2 + V_F + 1)
                f_block(i, 1, lambda c: None)

            with pe.Fori(0, NBLK // 2) as i:
                for b in range(2):
                    pe.wait_ge(dve_evac, i * 2 + (V_D - 1 + b) + 1)
                    for c in range(CF):
                        if KC * c % BT == 0:
                            pe.wait_ge(gul_ready, KC * c // BT + 1 + 1)
                        q = CHUNK_D + b * CF + c
                        tok_chunk(i * (2 * CF) + q, q % SLOTS, guH, guL, KC * c, b, c == 0, c == CF - 1)
                        if b == 1 and c == 4:
                            pe.wait_ge(dve_evac, i * 2 + (V_D + 1) + 1)
                            pe.wait_ge(fl_ready, i + NBLK + 1)
                            transposes(hb, 4).then_inc(htr_done, 1)

            def late_transposes(n, before):
                pe.wait_ge(dve_evac, V_D + n + 1 + 1)
                pe.wait_ge(fl_ready, before + 1)
                transposes(h3[:, :, n * NB:(n + 1) * NB], 4).then_inc(htr_done, 1)

            pe.wait_ge(pl_ready, 1)
            for n in range(NBLK):
                pe.wait_ge(dve_evac, V_D + NBLK - 1 + min(n, 1) + 1)
                if n >= 2:
                    pe.wait_ge(act_evac, A_P + n - 1)
                q = CHUNK_P + n
                tok_chunk(q, q % SLOTS, pH, pL, 0, n, True, True)
                if n == 0:
                    late_transposes(1, NBLK + 2)
            late_transposes(3, NBLK + 3)

            def e_block(q, n, first):
                for c in range(CB):
                    if first and c == 6:
                        pe.wait_ge(fl_ready, NBLK + 4 + 1)
                    tok_chunk(q + c, c % SLOTS, aH, aL, KC * c, n, c == 0, c == CB - 1,
                              e0_done if n == NBLK - 1 and c == CB - 1 else None)

            pe.wait_ge(fl_ready, NBLK + 3 + 1)
            for n in range(NBLK):
                pe.wait_ge(act_evac, A_P + 3 + n)
                e_block(CHUNK_E + n * CB, n, n == 0)


def blocks_of(np, w, chunk_rows):
    k, n = w.shape
    w = w.reshape(k // chunk_rows, KC, P, n // NB, NB)
    return w.transpose(3, 0, 2, 1, 4).reshape(n // NB, k // chunk_rows, P, KC * NB)


def kernel(**inputs):
    import numpy as np
    import concourse.bacc as bacc
    from concourse.bass_utils import run_bass_kernel_spmd

    a = {k: np.asarray(v) for k, v in inputs.items()}
    w_in = a["w_in"][0]
    da = 2 * D
    o_x, o_b, o_c, o_dt = da + D, da + 2 * D, da + 2 * D + GROUPS * P, da + 2 * D + 2 * GROUPS * P

    def cut(w):
        return blocks_of(np, w, KC * P)

    groups = np.concatenate([
        np.concatenate([w_in[:, o_x + g * GC:o_x + (g + 1) * GC], w_in[:, o_b + g * P:o_b + (g + 1) * P],
                        w_in[:, o_c + g * P:o_c + (g + 1) * P]], axis=1) for g in range(GROUPS)], axis=1)

    def pairs(first, second):
        return np.stack([cut(first), cut(second)], axis=1).reshape(-1, P, KC * NB)

    w_out, w_up = a["w_out"][0], a["w_up"][0]
    flat = lambda w: w.reshape(-1, P, KC * NB)
    stream = np.concatenate([
        flat(cut(w_in[:, da:da + D])), flat(cut(groups)), pairs(w_in[:, D:da], w_in[:, :D]),
        pairs(w_out[D:], w_out[:D]), pairs(w_up[:, :D_FF], w_up[:, D_FF:]), flat(cut(a["w_down"][0])),
        flat(cut(a["w_ple"][0])), flat(cut(a["w_ple_gate"][0]))])

    tiles = lambda vec: vec.reshape(-1, P).T
    conv = np.concatenate([a["conv_ssm_w"][0], a["conv_ssm_b"]])
    nbc = GROUPS * P
    conv = np.concatenate([
        conv[:, :D].reshape(5, GROUPS, 2, P), conv[:, D:D + nbc].reshape(5, GROUPS, 1, P),
        conv[:, D + nbc:].reshape(5, GROUPS, 1, P)], axis=2)
    convf = np.concatenate([a["conv_ffn_w"][0], a["conv_ffn_b"]]).reshape(4, 2 * KF, P)
    prm = np.concatenate([
        tiles(a["norm_mix_g"][0]), tiles(a["norm_ffn_g"][0]), tiles(a["norm_ple_g"][0]), tiles(a["norm_a_g"][0]),
        tiles(a["ssm_norm_g"][0]), a["b_s"][0].T, conv.transpose(3, 1, 2, 0).reshape(P, -1),
        convf.transpose(2, 1, 0).reshape(P, -1)], axis=1)
    arrays = {
        "x": a["x"][0],
        "xT": a["x"][0].T.reshape(KD, P, SEQ).transpose(1, 0, 2),
        "wstream": stream.reshape(CHUNKS, P, KC, NB),
        "wdt": w_in[:, o_dt:].reshape(KD, P, HEADS).transpose(1, 0, 2),
        "prm": prm,
        "rows": np.stack([a["dt_bias"][0], a["a_log"][0], a["d_skip"][0]]),
        "wsT": a["w_s"][0].reshape(NBLK, BT, P, P).transpose(0, 3, 1, 2),
        "ln": np.stack([a["ln_a_g"][0].reshape(NBLK, NB), a["ln_a_b"][0].reshape(NBLK, NB)], axis=1),
        "pT": a["p"][0, 0].T.reshape(KC, P, SEQ).transpose(1, 0, 2),
        "gf": a["norm_final_g"],
    }
    nc = bacc.Bacc("TRN2", target_bir_lowering=False, num_devices=1)
    arrays = {"in_" + k: np.ascontiguousarray(v) for k, v in arrays.items()}
    args = [nc.dram_tensor(k, v.shape, F32, kind="ExternalInput").ap() for k, v in arrays.items()]
    out = nc.dram_tensor("out", (SEQ, D), F32, kind="ExternalOutput").ap()
    build(nc, *args, out)
    got = run_bass_kernel_spmd(nc, [arrays], core_ids=[0]).results[0]["out"]
    return got.reshape(1, SEQ, D)
```
